# Optimizing a Trainium2 kernel written in Bass

```python
import jax, jax.numpy as jnp
from jax import lax
import numpy as np

D_MODEL = 2048
BATCH = 1
SEQ = 256
DEPTH = 1

D_MIX = D_MODEL
HEAD_DIM = 128
ATTN_WIDTH = D_MIX // 2
N_ATTN_HEADS = ATTN_WIDTH // HEAD_DIM
ROPE_DIM = HEAD_DIM // 4
ROPE_THETA = 500000.0
DILATED_PATTERNS = ((128, 1), (512, 4), (2048, 16))
ATTN_BLOCK = 128
RNN_WIDTH = D_MIX - ATTN_WIDTH
RNN_BLOCKS = 16
RNN_BLOCK_DIM = RNN_WIDTH // RNN_BLOCKS
CONV_WIDTH = 4
RGLRU_C = 8.0
PEER_HEADS = 8
PEER_NKEYS = 128
PEER_EXPERTS = PEER_NKEYS * PEER_NKEYS
PEER_TOPK = 16
PEER_KEY_DIM = 128
PEER_TOKEN_BLOCK = 128
PLE_DIM = 256
PROJ_IN = 3 * ATTN_WIDTH + 2 * RNN_WIDTH
EPS = 1e-6

kernel_name = "hybrid_dilated_attn_rglru_peer_block"

def rmsnorm(x, g):
    xf = x.astype(jnp.float32)
    y = xf * lax.rsqrt(jnp.mean(xf * xf, axis=-1, keepdims=True) + EPS)
    return (y * g.astype(jnp.float32)).astype(x.dtype)

def partial_rope(t, positions):
    half = ROPE_DIM // 2
    inv_freq = ROPE_THETA ** (-jnp.arange(half, dtype=jnp.float32) * 2.0 / ROPE_DIM)
    ang = positions.astype(jnp.float32)[..., None] * inv_freq
    cos = jnp.cos(ang)[:, :, None, :]
    sin = jnp.sin(ang)[:, :, None, :]
    tf = t.astype(jnp.float32)
    x1 = tf[..., :half]
    x2 = tf[..., half:ROPE_DIM]
    out = jnp.concatenate([x1 * cos - x2 * sin, x2 * cos + x1 * sin, tf[..., ROPE_DIM:]], axis=-1)
    return out.astype(t.dtype)

def dilated_window_attention(q, k, v, window, dilation):
    B, Sp, H, Dh = q.shape
    steps = window // dilation
    assert steps <= ATTN_BLOCK
    Q = Sp // dilation
    nb = Q // ATTN_BLOCK

    def to_blocks(t):
        t = t.reshape(B, Q, dilation, H, Dh).transpose(0, 3, 2, 1, 4)
        return t.reshape(B, H, dilation, nb, ATTN_BLOCK, Dh)

    def with_prev(t):
        prev = jnp.pad(t, ((0, 0), (0, 0), (0, 0), (1, 0), (0, 0), (0, 0)))[:, :, :, :-1]
        return jnp.concatenate([prev, t], axis=4)

    qb = to_blocks(q)
    kk = with_prev(to_blocks(k))
    vv = with_prev(to_blocks(v))
    s = jnp.einsum('bhrnqd,bhrnkd->bhrnqk', qb, kk,
                   preferred_element_type=jnp.float32) * (Dh ** -0.5)
    qi = jnp.arange(ATTN_BLOCK)[:, None]
    kj = jnp.arange(2 * ATTN_BLOCK)[None, :]
    dist = ATTN_BLOCK + qi - kj
    band = (dist >= 0) & (dist <= steps)
    has_prev = (jnp.arange(nb) > 0)[:, None, None] | (kj >= ATTN_BLOCK)[None]
    mask = band[None] & has_prev
    s = jnp.where(mask, s, -jnp.inf)
    m = jnp.max(s, axis=-1)
    e = jnp.exp(s - m[..., None])
    l = jnp.sum(e, axis=-1)
    o = jnp.einsum('bhrnqk,bhrnkd->bhrnqd', e, vv.astype(jnp.float32)) / l[..., None]
    o = o.reshape(B, H, dilation, Q, Dh).transpose(0, 3, 2, 1, 4).reshape(B, Sp, H, Dh)

    def stat_back(t):
        return t.reshape(B, H, dilation, Q).transpose(0, 3, 2, 1).reshape(B, Sp, H)

    return o, stat_back(m), stat_back(l)

def attention_mixer(q, k, v, positions):
    B, S, H, Dh = q.shape
    q = partial_rope(q, positions)
    k = partial_rope(k, positions)
    span = ATTN_BLOCK * int(np.lcm.reduce(np.array([d for _, d in DILATED_PATTERNS])))
    Sp = -(-S // span) * span
    pad = ((0, 0), (0, Sp - S), (0, 0), (0, 0))
    q, k, v = jnp.pad(q, pad), jnp.pad(k, pad), jnp.pad(v, pad)
    outs = [dilated_window_attention(q, k, v, w, d) for w, d in DILATED_PATTERNS]
    o_all = jnp.stack([o for o, _, _ in outs])
    m_all = jnp.stack([m for _, m, _ in outs])
    l_all = jnp.stack([l for _, _, l in outs])
    m_max = jnp.max(m_all, axis=0)
    wts = l_all * jnp.exp(m_all - m_max)
    o = jnp.sum(wts[..., None] * o_all, axis=0) / jnp.sum(wts, axis=0)[..., None]
    return o[:, :S].reshape(B, S, H * Dh)

def causal_depthwise_conv(x, w, b):
    S = x.shape[1]
    xp = jnp.pad(x, ((0, 0), (CONV_WIDTH - 1, 0), (0, 0)))
    y = b
    for tap in range(CONV_WIDTH):
        y = y + xp[:, tap:tap + S] * w[tap]
    return y

def rglru(x, w_a, b_a, w_x, b_x, lam):
    B, S, W = x.shape
    xb = x.reshape(B, S, RNN_BLOCKS, RNN_BLOCK_DIM)
    r = jax.nn.sigmoid(jnp.einsum('bsnd,nde->bsne', xb, w_a).reshape(B, S, W).astype(jnp.float32) + b_a)
    i = jax.nn.sigmoid(jnp.einsum('bsnd,nde->bsne', xb, w_x).reshape(B, S, W).astype(jnp.float32) + b_x)
    log_a = -RGLRU_C * r * jax.nn.softplus(-lam.astype(jnp.float32))
    a = jnp.exp(log_a)
    mult = jnp.sqrt(-jnp.expm1(2.0 * log_a))
    u = mult * i * x.astype(jnp.float32)

    def combine(c1, c2):
        a1, b1 = c1
        a2, b2 = c2
        return a1 * a2, a2 * b1 + b2

    _, h = lax.associative_scan(combine, (a, u), axis=1)
    return h.astype(x.dtype)

def peer_ffn(xn, w_q, subkeys, u, v):
    B, S, D = xn.shape
    T = B * S
    xt = xn.reshape(T // PEER_TOKEN_BLOCK, PEER_TOKEN_BLOCK, D)

    def block(xb):
        q = (xb @ w_q).reshape(PEER_TOKEN_BLOCK, PEER_HEADS, 2, PEER_KEY_DIM)
        s = jnp.einsum('thcd,hckd->thck', q, subkeys, preferred_element_type=jnp.float32)
        s_top, i_top = lax.top_k(s, PEER_TOPK)
        cand = (s_top[:, :, 0, :, None] + s_top[:, :, 1, None, :]).reshape(
            PEER_TOKEN_BLOCK, PEER_HEADS, PEER_TOPK * PEER_TOPK)
        best, pos = lax.top_k(cand, PEER_TOPK)
        i1 = jnp.take_along_axis(i_top[:, :, 0], pos // PEER_TOPK, axis=-1)
        i2 = jnp.take_along_axis(i_top[:, :, 1], pos % PEER_TOPK, axis=-1)
        expert = i1 * PEER_NKEYS + i2
        g = jax.nn.softmax(best, axis=-1)
        act = jax.nn.gelu(jnp.einsum('thkd,td->thk', u[expert], xb,
                                     preferred_element_type=jnp.float32))
        return jnp.einsum('thk,thkd->td', (g * act).astype(xb.dtype), v[expert])

    return lax.map(block, xt).reshape(B, S, D)

def setup_inputs(seed: int = 0) -> dict:
    key = jax.random.key(seed)
    ks = jax.random.split(key, 26)

    def nrm(k, shape, scale):
        return jax.random.normal(k, shape, jnp.float32) * scale

    def gain(k, shape):
        return 1.0 + 0.05 * jax.random.normal(k, shape, jnp.float32)

    a0 = jax.random.uniform(ks[11], (DEPTH, RNN_WIDTH), jnp.float32, 0.9, 0.999) ** (1.0 / RGLRU_C)
    return {
        "x": nrm(ks[0], (BATCH, SEQ, D_MODEL), 1.0),
        "p": nrm(ks[1], (DEPTH, BATCH, SEQ, PLE_DIM), 1.0),
        "positions": jnp.broadcast_to(jnp.arange(SEQ, dtype=jnp.int32), (BATCH, SEQ)),
        "mix_norm": gain(ks[2], (DEPTH, D_MODEL)),
        "w_in": nrm(ks[3], (DEPTH, D_MODEL, PROJ_IN), D_MODEL ** -0.5),
        "conv_w": nrm(ks[4], (DEPTH, CONV_WIDTH, RNN_WIDTH), CONV_WIDTH ** -0.5),
        "conv_b": nrm(ks[5], (DEPTH, RNN_WIDTH), 0.02),
        "rg_wa": nrm(ks[6], (DEPTH, RNN_BLOCKS, RNN_BLOCK_DIM, RNN_BLOCK_DIM), RNN_BLOCK_DIM ** -0.5),
        "rg_ba": nrm(ks[7], (DEPTH, RNN_WIDTH), 0.02),
        "rg_wx": nrm(ks[8], (DEPTH, RNN_BLOCKS, RNN_BLOCK_DIM, RNN_BLOCK_DIM), RNN_BLOCK_DIM ** -0.5),
        "rg_bx": nrm(ks[9], (DEPTH, RNN_WIDTH), 0.02),
        "rg_lambda": jnp.log(a0) - jnp.log1p(-a0),
        "attn_out_norm": gain(ks[12], (DEPTH, ATTN_WIDTH)),
        "rnn_out_norm": gain(ks[13], (DEPTH, RNN_WIDTH)),
        "w_out": nrm(ks[14], (DEPTH, D_MIX, D_MODEL), D_MIX ** -0.5),
        "ffn_norm": gain(ks[15], (DEPTH, D_MODEL)),
        "peer_wq": nrm(ks[16], (DEPTH, D_MODEL, PEER_HEADS * 2 * PEER_KEY_DIM), D_MODEL ** -0.5),
        "peer_subkeys": nrm(ks[17], (DEPTH, PEER_HEADS, 2, PEER_NKEYS, PEER_KEY_DIM), PEER_KEY_DIM ** -0.5),
        "peer_u": nrm(ks[18], (DEPTH, PEER_EXPERTS, D_MODEL), D_MODEL ** -0.5),
        "peer_v": nrm(ks[19], (DEPTH, PEER_EXPERTS, D_MODEL), 0.5),
        "ple_norm": gain(ks[20], (DEPTH, D_MODEL)),
        "ple_w_gate": nrm(ks[21], (DEPTH, D_MODEL, D_MODEL), D_MODEL ** -0.5),
        "ple_b_gate": nrm(ks[22], (DEPTH, D_MODEL), 0.02),
        "ple_proj": nrm(ks[23], (DEPTH, PLE_DIM, D_MODEL), PLE_DIM ** -0.5),
        "final_norm": gain(ks[24], (D_MODEL,)),
    }

def reference(x, p, positions, mix_norm, w_in, conv_w, conv_b, rg_wa, rg_ba, rg_wx, rg_bx,
              rg_lambda, attn_out_norm, rnn_out_norm, w_out, ffn_norm, peer_wq, peer_subkeys,
              peer_u, peer_v, ple_norm, ple_w_gate, ple_b_gate, ple_proj, final_norm):
    B, S, _ = x.shape
    A = ATTN_WIDTH
    h = x
    for i in range(DEPTH):
        xn = rmsnorm(h, mix_norm[i])
        proj = xn @ w_in[i]
        q = proj[..., 0:A].reshape(B, S, N_ATTN_HEADS, HEAD_DIM)
        k = proj[..., A:2 * A].reshape(B, S, N_ATTN_HEADS, HEAD_DIM)
        v = proj[..., 2 * A:3 * A].reshape(B, S, N_ATTN_HEADS, HEAD_DIM)
        xr = proj[..., 3 * A:3 * A + RNN_WIDTH]
        gate = proj[..., 3 * A + RNN_WIDTH:]
        attn = attention_mixer(q, k, v, positions).astype(h.dtype)
        xr = causal_depthwise_conv(xr, conv_w[i], conv_b[i])
        rnn = rglru(xr, rg_wa[i], rg_ba[i], rg_wx[i], rg_bx[i], rg_lambda[i]) * jax.nn.gelu(gate)
        mixed = jnp.concatenate([rmsnorm(attn, attn_out_norm[i]), rmsnorm(rnn, rnn_out_norm[i])], axis=-1)
        h = h + mixed @ w_out[i]
        hn = rmsnorm(h, ffn_norm[i])
        h = h + peer_ffn(hn, peer_wq[i], peer_subkeys[i], peer_u[i], peer_v[i])
        g = jax.nn.sigmoid(rmsnorm(h, ple_norm[i]) @ ple_w_gate[i] + ple_b_gate[i])
        h = h + g * (p[i] @ ple_proj[i])
    return rmsnorm(h, final_norm)


_drawn_inputs = setup_inputs


def setup_inputs(seed=0):
    import zlib

    import numpy as np

    out = dict(_drawn_inputs(seed))
    spreads = {}
    factors = {'rg_ba': 6.969, 'rg_bx': 5.321, 'ple_norm': 8.0, 'ple_b_gate': 49.452}
    for name, (base, spread) in spreads.items():
        noise = np.random.default_rng([zlib.crc32(name.encode()), seed]).standard_normal(out[name].shape)
        drawn = base * np.exp(spread * noise) if base else spread * noise
        out[name] = __import__('jax').numpy.asarray(drawn.astype(out[name].dtype))
    for name, factor in factors.items():
        out[name] = (out[name] * factor).astype(out[name].dtype)
    return out
```

```python
from contextlib import ExitStack

import numpy as np
import concourse.bass as bass
from concourse import mybir

ALU = mybir.AluOpType
ACT = mybir.ActivationFunctionType
AX_X = mybir.AxisListType.X
F32 = mybir.dt.float32
BF16 = mybir.dt.bfloat16
F32R = mybir.dt.float32r
I32 = mybir.dt.int32
U32 = mybir.dt.uint32

P = 128
S = 256
TB = S // P
D = 2048
KC = D // P
HEADS = 8
A = HEADS * P
RC = 8
ROT = 16
SCALE = float(P) ** -0.5
EPS = 1e-6
TAPS = 4
RGLRU_C = 8.0
PH = 8
HC = 2 * PH
KEYS = 128
TOPK = 16
SLOTS = PH * TOPK
NEG = -3.0e38
MASKED = -1.0e30

UW = 1024
RAW = 8
CV = 4
GE = 8
NG = 128 // GE
AHEAD = 5
U_QKV = 0
U_XR = U_QKV + 48
U_GATE = U_XR + 16
U_OUTA = U_GATE + 16
U_OUTR = U_OUTA + 16
U_WQ = U_OUTR + 16
U_U0 = U_WQ + 32
U_VU = U_U0 + 16 * AHEAD
U_V1 = U_VU + 32 * (NG - AHEAD)
U_PROJ = U_V1 + 16 * AHEAD
U_PLE = U_PROJ + 4
UNITS = U_PLE + 32
M_OUTA, M_OUTR, M_V = 6, 10, 14
M_PROJ = M_V + 4 * NG
M_PLE = M_PROJ + 4
C_MIX, C_FFN, C_PLE = 0, 16, 32
C_GA, C_GR, C_CW, C_CB, C_BA, C_BX, C_LAM = 48, 56, 64, 96, 104, 112, 120
C_FREQ = 128
C_END = 144
TAU = 6.283185307179586
TAU1 = 6.28125
TAU2 = 0.0019350051879882812
TAU3 = 3.019915981956753e-07
ROUND = 12582912.0


def build(nc, stream, x, positions, cols, masks, w_a, w_x, subkeys, p_t, b_gate, final_norm, iota, ident, g_dram, out):
    ctx = ExitStack()
    with ctx:
        def sb(name, shape, dt=F32):
            return ctx.enter_context(nc.sbuf_tensor(name, shape, dt))

        def sem(name):
            return ctx.enter_context(nc.semaphore(name))

        bank = [ctx.enter_context(nc.psum_tensor(f"bank{i}", [P, 512], F32)) for i in range(8)]
        xop = sb("xop", [P, KC, 2, S], F32R)
        with nc.sbuf_tensor("atop", [P, GE, 2, S], F32R) as atop:
            pass
        with nc.sbuf_tensor("hot", [P, 2, 4, P, 8], BF16) as hot:
            pass
        wop = sb("wop", [P, GE, 2, S], F32R)
        pop = sb("pop", [P, 2, 2, S], F32R)
        hi = sb("hi", [P, CV, UW], F32R)
        lo = sb("lo", [P, CV, UW], F32R)
        raw = sb("raw", [P, RAW, UW])
        hres = sb("hres", [P, TB, D])
        arena = sb("arena", [P, 14336])
        idn = sb("idn", [P, P])
        iot = sb("iot", [P, P])
        col = sb("col", [P, C_END])
        ones = sb("ones", [P, P])
        sml = sb("sml", [P, 512])
        posi = sb("posi", [P, TB], I32)
        tmp = sb("tmp", [P, 2, 2, S])
        pick = sb("pick", [P, 2, 3, P])
        pos = sb("pos", [P, 2, P], U32)
        keyb = sb("keyb", [P, 2, S], BF16)
        gpart = sb("gpart", [P, 3, S], BF16)
        grest = sb("grest", [P, S])

        sqt, sqsum = tmp[:, 0], tmp[:, 1, 0]
        qt, tkw = tmp[:, 0], tmp[:, 1]

        ar = arena
        xs = ar[:, 0:4096].rearrange("p (b d) -> p b d", b=TB)
        qk = xs
        vsb = ar[:, 4096:6144].rearrange("p (b d) -> p b d", b=TB)
        qkt = ar[:, 6144:7168].rearrange("p (n q t) -> p n q t", n=2, q=2)
        madd, mcnt = ar[:, 7168:7552], ar[:, 7552:7936]
        sm = ar[:, 7936:8704].rearrange("p (n k) -> p n k", n=2)
        pt = ar[:, 8704:9472].rearrange("p (n k) -> p n k", n=2)
        at = ar[:, 9472:9984].rearrange("p (n t) -> p n t", n=2)
        xr = ar[:, 10240:12288].rearrange("p (c t) -> p c t", c=RC)
        gate = ar[:, 12288:14336].rearrange("p (c t) -> p c t", c=RC)
        xc = ar[:, 0:2048].rearrange("p (c t) -> p c t", c=RC)
        rg = ar[:, 2048:4096].rearrange("p (c t) -> p c t", c=RC)
        bd = ar[:, 4096:6144].rearrange("p (m c d) -> p m c d", m=2, c=RC)
        ig = ar[:, 6144:8192].rearrange("p (c t) -> p c t", c=RC)
        av = ar[:, 8192:10240].rearrange("p (c t) -> p c t", c=RC)
        naive = ar[:, 4096:6144]
        poly = ar[:, 10240:12288]
        msk = ar[:, 0:2048]
        skey = ar[:, 4096:6144].rearrange("p (n k) -> p n k", n=HC)
        tks = ar[:, 8192:8704].rearrange("p (b n k) -> p b n k", b=TB, n=HC)
        tki = ar[:, 8704:9216].bitcast(U32).rearrange("p (b n k) -> p b n k", b=TB, n=HC)
        tkf = ar[:, 9216:9728].rearrange("p (b n k) -> p b n k", b=TB, n=HC)
        best = ar[:, 9728:9984].rearrange("p (b n k) -> p b n k", b=TB, n=PH)
        ex = ar[:, 9984:10240].rearrange("p (b n) -> p b n", b=TB)
        cand = ar[:, 10240:12288].rearrange("p (n a b) -> p n a b", n=PH, a=TOPK)
        eq = ar[:, 12288:14336].rearrange("p (n a b) -> p n a b", n=PH, a=TOPK)
        stg = [ar[:, 8192:10240], ar[:, 12288:14336]]
        gt = ar[:, 10240:12288]
        irep = ar[:, 10240:10752].bitcast(BF16).rearrange("p (i t) -> p i t", t=8)
        eqb = ar[:, 10752:11776].bitcast(BF16).rearrange("p (n i t) -> p n i t", n=2, t=8)
        fnb = ar[:, 8192:10240]
        pp = ar[:, 4096:8192].rearrange("p (b d) -> p b d", b=TB)
        brow = ar[0:1, 10240:12288]
        junk = ar[:, 0:4096].rearrange("p (n b d) -> p n b d", n=4, b=TB)
        sg = ar[:, 12288:14336].rearrange("p (n b d) -> p n b d", n=2, b=TB)
        praw = ar[:, 10240:10752].rearrange("p (c t) -> p c t", c=2)
        ring = AHEAD * GE * S

        raw_in = [sem(f"raw_in{i}") for i in range(RAW)]
        hi_done, lo_done, unit_used = sem("hi_done"), sem("lo_done"), sem("unit_used")
        const_in, x_in, bd_in, sk_in, late_in = sem("const_in"), sem("x_in"), sem("bd_in"), sem("sk_in"), sem("late_in")
        mm_free, st_free, ua_free = sem("mm_free"), sem("st_free"), sem("ua_free")
        ssq_done, xs_done = sem("ssq_done"), sem("xs_done")
        xt_ready, xt_gain, xt_split = sem("xt_ready"), sem("xt_gain"), sem("xt_split")
        dve_step = sem("dve_step")
        trig_ready, sin_done = sem("trig_ready"), sem("sin_done")
        rope_done = sem("rope_done")
        ht_ready, ht_copied = sem("ht_ready"), sem("ht_copied")
        sc_ready, sc_read = sem("sc_ready"), sem("sc_read")
        nmx_done, exp_done, prob_done = sem("nmx_done"), sem("exp_done"), sem("prob_done")
        pt_ready, pt_copied = sem("pt_ready"), sem("pt_copied")
        pv_ready, pv_gain, at_split = sem("pv_ready"), sem("pv_gain"), sem("at_split")
        asum_ready, asum_out = sem("asum_ready"), sem("asum_out")
        bd_zero, conv_done, bd_ready = sem("bd_zero"), sem("conv_done"), sem("bd_ready")
        gates_done, l_done, a_done = sem("gates_done"), sem("l_done"), sem("a_done")
        rnn_split, rsum_ready, rsum_out = sem("rnn_split"), sem("rsum_ready"), sem("rsum_out")
        key_ready, key_read = sem("key_ready"), sem("key_read")
        bm_done, eg_done, picked = sem("bm_done"), sem("eg_done"), sem("picked")
        sel_ready, sel_read = sem("sel_ready"), sem("sel_read")
        hot_done, g_ready, g_copied = sem("hot_done"), sem("g_ready"), sem("g_copied")
        g_out = [sem("g_out0"), sem("g_out1")]
        g_in, g_used, wexp_done = sem("g_in"), sem("g_used"), sem("wexp_done")
        sig_done, ple_done, y_done, out_done = sem("sig_done"), sem("ple_done"), sem("y_done"), sem("out_done")
        mean_done, root_done = sem("mean_done"), sem("root_done")
        one_done, pop_done, lam_done, gelu_done = sem("one_done"), sem("pop_done"), sem("lam_done"), sem("gelu_done")
        rate_exp, rm_done, rm_gain, pj_done = sem("rate_exp"), sem("rm_done"), sem("rm_gain"), sem("pj_done")

        N_CONST = 7

        block = ctx.enter_context(nc.Block())

        @block.sync
        def _(sp):
            for b in range(RAW):
                sp.dma_start(raw[:, b, :], stream[b]).then_inc(raw_in[b], 16)
            with sp.Fori(1, UNITS // RAW) as i:
                for b in range(RAW):
                    sp.wait_ge(lo_done, RAW * i + b - RAW + 1)
                    sp.dma_start(raw[:, b, :], stream[RAW * i + b]).then_inc(raw_in[b], 16)
            for n in range(UNITS // RAW * RAW, UNITS):
                sp.wait_ge(lo_done, n - RAW + 1)
                sp.dma_start(raw[:, n % RAW, :], stream[n]).then_inc(raw_in[n % RAW], 16)
            sp.wait_ge(y_done, TB)
            sp.dma_start(out.rearrange("(b p) d -> p b d", p=P), xs).then_inc(out_done, 16)
            sp.wait_ge(out_done, 16)

        @block.gpsimd
        def _(pool):
            pool.memset(ones[:], 1.0).then_inc(one_done, 1)
            with pool.Fori(0, UNITS // CV // 2) as i:
                for b in range(2 * CV):
                    pool.wait_ge(hi_done, 2 * CV * i + b + 1)
                    pool.tensor_tensor(lo[:, b % CV, :], raw[:, b, :], hi[:, b % CV, :].bitcast(F32),
                                       ALU.subtract).then_inc(lo_done, 1)
            for n in range(UNITS // (2 * CV) * 2 * CV, UNITS):
                pool.wait_ge(hi_done, n + 1)
                pool.tensor_tensor(lo[:, n % CV, :], raw[:, n % RAW, :], hi[:, n % CV, :].bitcast(F32),
                                   ALU.subtract).then_inc(lo_done, 1)

        @block.scalar
        def _(act):
            made = [0]

            def round_unit(n, k, loop):
                act.wait_ge(raw_in[k], 2 * (n - k) + 16)
                if loop or n >= CV:
                    act.wait_ge(unit_used, n - CV + 1)
                act.activation(hi[:, k % CV, :], raw[:, k, :], ACT.Copy).then_inc(hi_done, 1)

            def round_to(n):
                while made[0] <= min(n, UNITS - 1):
                    round_unit(made[0], made[0] % RAW, False)
                    made[0] += 1

            act.dma_start(hres[:, 0, :], x[0:P, :]).then_inc(x_in, 16)
            act.dma_start(hres[:, 1, :], x[P:S, :]).then_inc(x_in, 16)
            act.dma_start(col[:], cols).then_inc(const_in, 16)
            act.dma_start(idn[:], ident).then_inc(const_in, 16)
            act.dma_start(posi[:], positions).then_inc(const_in, 16)
            act.dma_start(madd, masks[0]).then_inc(const_in, 16)
            act.dma_start(mcnt, masks[1]).then_inc(const_in, 16)
            act.dma_start(iot[:], iota).then_inc(const_in, 16)
            act.dma_start(praw, p_t).then_inc(const_in, 16)

            def root(n, at_):
                act.wait_ge(mean_done, n + 1)
                act.activation(at_, at_, ACT.Sqrt).then_inc(root_done, 1)

            def squares(n):
                for b in range(TB):
                    act.activation(xs[:, b, :], hres[:, b, :], ACT.Square,
                                   accum_out=sml[:, 2 * n + b:2 * n + b + 1]).then_inc(ssq_done, 1)

            def gains(n, c0):
                for k in range(KC):
                    if k % 2 == 0:
                        act.wait_ge(xt_ready, 8 * n + k // 2 + 1)
                        if k // 2 >= 2:
                            act.wait_ge(xt_split, 8 * n + k // 2 - 1)
                    act.activation(tmp[:, k // 2 % 2, k % 2, :], bank[4 + k // 2 % 4][:, k % 2 * S:k % 2 * S + S],
                                   ACT.Copy, scale=col[:, c0 + k:c0 + k + 1]).then_inc(xt_gain, 1)

            act.wait_ge(x_in, 32)
            squares(0)
            root(0, sml[:, 8:10])
            act.wait_ge(const_in, 16 * N_CONST)
            act.wait_ge(lam_done, 1)
            act.activation(sml[:, 272:280], sml[:, 264:272], ACT.Exp, scale=-1.0).then_inc(rate_exp, 1)
            round_to(CV - 1)
            gains(0, C_MIX)
            act.wait_ge(trig_ready, 1)
            act.activation(sml[:, 128:192], sml[:, 64:128], ACT.Sin).then_inc(sin_done, 1)
            for m in range(6):
                round_to(8 * m + 7 + CV - 1)
                act.wait_ge(unit_used, 8 * m + 8)
                for b in range(TB):
                    dst = qk[:, b, 512 * m:512 * m + 512] if m < 4 else vsb[:, b, 512 * (m - 4):512 * (m - 3)]
                    ins = act.activation(dst, bank[m % 2 * 2 + b][:], ACT.Copy)
                ins.then_inc(mm_free, 1)

            def tall(j):
                round_to(U_XR + 2 * j + 1 + CV - 1)
                act.wait_ge(unit_used, U_XR + 2 * j + 2)
                if j == 0:
                    act.wait_ge(pop_done, 1)
                dst = xr[:, j, :] if j < RC else gate[:, j - RC, :]
                act.activation(dst, bank[j % 2][:, 0:S], ACT.Copy).then_inc(st_free, 1)

            for i in range(HEADS + 3):
                if i < 8:
                    tall(2 * i)
                h = i - 1
                if 0 <= h < HEADS:
                    act.wait_ge(nmx_done, h + 1)
                    act.activation(sm[:, h % 2, 0:P], sm[:, h % 2, 0:P], ACT.Exp, scale=SCALE,
                                   bias=sml[:, 16 + 2 * (h % 2):17 + 2 * (h % 2)])
                    act.activation(sm[:, h % 2, P:384], sm[:, h % 2, P:384], ACT.Exp, scale=SCALE,
                                   bias=sml[:, 17 + 2 * (h % 2):18 + 2 * (h % 2)]).then_inc(exp_done, 1)
                h = i - 2
                if 0 <= h < HEADS:
                    act.wait_ge(pt_ready, h + 1)
                    if h >= 2:
                        act.wait_ge(pv_ready, h - 1)
                    act.activation(pt[:, h % 2, :], bank[6][:, 0:384], ACT.Copy).then_inc(pt_copied, 1)
                h = i - 3
                if 0 <= h < HEADS:
                    act.wait_ge(pv_ready, h + 1)
                    if h >= 2:
                        act.wait_ge(at_split, h - 1)
                    act.activation(at[:, h % 2, :], bank[7][:, 0:S], ACT.Copy,
                                   scale=col[:, C_GA + h:C_GA + h + 1])
                    act.activation(sqt[:, h % 2, :], bank[7][:, 0:S], ACT.Square).then_inc(pv_gain, 1)
                if i < 8:
                    tall(2 * i + 1)
            act.wait_ge(st_free, 16)
            act.activation(ar[:, 12288:14336], ar[:, 12288:14336], ACT.Gelu_apprx_tanh).then_inc(gelu_done, 1)
            act.wait_ge(bd_zero, 1)
            for m, w in enumerate((w_a, w_x)):
                for e in range(2):
                    act.dma_start(bd[64 * e:64 * e + 64, m, :, 64 * e:64 * e + 64],
                                  w.rearrange("(c e) i o -> e i c o", e=2)[e]).then_inc(bd_in, 16)

            round_to(U_OUTA + CV - 1)
            root(1, sml[:, 24:26])
            round_to(U_OUTA + 7 + CV - 1)
            for n in range(2 * RC):
                m, c = n // RC, n % RC
                act.wait_ge(bd_ready, n + 1)
                act.activation((rg, ig)[m][:, c, :], bank[4 + n % 4][:, 0:S], ACT.Sigmoid,
                               bias=col[:, (C_BA, C_BX)[m] + c:(C_BA, C_BX)[m] + c + 1]).then_inc(gates_done, 1)
            round_to(U_OUTA + 11 + CV - 1)
            act.wait_ge(l_done, 1)
            act.activation(ar[:, 8192:10240], ar[:, 2048:4096], ACT.Exp, scale=-1.0).then_inc(a_done, 1)
            round_to(U_OUTA + 15 + CV - 1)
            root(2, naive)
            act.wait_ge(rm_done, 1)
            for c in range(RC):
                act.activation(ig[:, c, :], gate[:, c, :], ACT.Copy,
                               scale=col[:, C_GR + c:C_GR + c + 1]).then_inc(rm_gain, 1)
            act.activation(naive, ar[:, 12288:14336], ACT.Square).then_inc(rm_gain, 1)
            root(3, sml[:, 26:28])
            round_to(U_OUTR + 15 + CV - 1)
            act.wait_ge(mm_free, M_V)
            act.dma_start(ar[:, 4096:6144], subkeys).then_inc(sk_in, 16)
            squares(1)
            root(4, sml[:, 10:12])
            gains(1, C_FFN)
            for j in range(HC):
                round_to(U_WQ + 2 * j + 1 + CV - 1)
                act.wait_ge(unit_used, U_WQ + 2 * j + 2)
                if j == 0:
                    act.wait_ge(xt_split, 16)
                if j >= 2:
                    act.wait_ge(key_ready, j - 1)
                act.activation(qt[:, j % 2, :], bank[j % 2][:, 0:S], ACT.Copy).then_inc(st_free, 1)

            def gelu_tile(g, j, n0):
                act.wait_ge(unit_used, n0 + 2 * j + 2)
                start = g % AHEAD * (GE * S) + j * S
                act.activation(ar[:, bass.ds(start, S)] if not isinstance(start, int) else ar[:, start:start + S], bank[4 + j % 2][:, 0:S],
                               ACT.Gelu_apprx_tanh).then_inc(ua_free, 1)

            def ahead(g):
                n0 = U_U0 + 2 * GE * g
                for j in range(GE):
                    for e in range(2):
                        off = 2 * j + e + CV - 1
                        round_unit(n0 + off, off % RAW, True)
                    gelu_tile(g, j, n0)

            act.wait_ge(key_ready, HC)
            with act.Fori(0, 2) as g:
                ahead(g)
            act.wait_ge(bm_done, TB)
            act.activation(ex, ex, ACT.Exp).then_inc(eg_done, 1)

            def spread(g, j, first):
                n0, c = U_U0 + 2 * GE * g, GE * (g - 2) + j
                for e in range(2):
                    off = 2 * j + e + CV - 1
                    round_unit(n0 + off, off % RAW, True)
                gelu_tile(g, j, n0)
                b = j % 2
                for s in range(4):
                    act.wait_ge(g_ready, 4 * c + s + 1)
                    if s == 0 and not (first and j < 2):
                        act.wait_ge(g_out[b], 8 * (c - b))
                    act.activation(stg[b].rearrange("p (i t) -> p t i", t=16)[:, 4 * s:4 * s + 4, :],
                                   bank[s][:].rearrange("p (t i) -> p t i", t=4), ACT.Copy).then_inc(g_copied, 1)
                act.wait_ge(g_copied, 4 * c + 4)
                act.dma_start(g_dram[:, :, c * P:c * P + P].rearrange("g p x -> p g x") if isinstance(c, int)
                              else g_dram[:, :, bass.ds(c * P, P)].rearrange("g p x -> p g x"),
                              stg[b].rearrange("p (g x) -> p g x", g=NG)).then_inc(g_out[b], 16)

            for j in range(GE):
                spread(2, j, True)
            for j in range(GE):
                spread(3, j, False)
            act.wait_ge(g_out[0], 128)
            act.wait_ge(g_out[1], 128)
            act.dma_start(gt, g_dram[0]).then_inc(g_in, 16)
            ahead(AHEAD - 1)

            def v_units(n0):
                for off in range(CV - 1, 16 + CV - 1):
                    round_unit(n0 + off, off % RAW, True)

            def next_weights(g):
                act.wait_ge(g_used, g)
                act.dma_start(gt, g_dram[bass.ds(g, 1)].rearrange("g p x -> p (g x)")).then_inc(g_in, 16)

            with act.Fori(0, NG - AHEAD) as g:
                next_weights(g + 1)
                n0 = U_VU + 32 * g
                v_units(n0)
                for j in range(GE):
                    for e in range(2):
                        off = 16 + 2 * j + e + CV - 1
                        round_unit(n0 + off, off % RAW, True)
                    gelu_tile(g + AHEAD, j, n0 + 16)
            with act.Fori(NG - AHEAD, NG - 1) as g:
                next_weights(g + 1)
                v_units(U_V1 + 16 * (g - (NG - AHEAD)))
            for off in range(CV - 1, 16 + CV - 1):
                round_unit(U_V1 + 16 * (AHEAD - 1) + off, off % RAW, False)
            made[0] = U_PROJ + CV - 1

            act.wait_ge(mm_free, M_PROJ)
            act.dma_start(fnb, final_norm).then_inc(late_in, 16)
            act.dma_start(brow, b_gate).then_inc(late_in, 16)
            squares(2)
            root(5, sml[:, 12:14])
            round_to(U_PROJ + 3)
            for m in range(4):
                act.wait_ge(unit_used, U_PROJ + m + 1)
                for b in range(TB):
                    ins = act.activation(pp[:, b, 512 * m:512 * m + 512], bank[m % 2 * 2 + b][:], ACT.Copy)
                ins.then_inc(mm_free, 1)
                round_to(U_PROJ + 4 + m)
            gains(2, C_PLE)
            for m in range(4):
                round_to(U_PLE + 8 * m + 7 + CV - 1)
                act.wait_ge(unit_used, U_PLE + 8 * m + 8)
                if m >= 2:
                    act.wait_ge(ple_done, m - 1)
                for b in range(TB):
                    ins = act.activation(sg[:, m % 2, b, :], bank[m % 2 * 2 + b][:], ACT.Sigmoid)
                ins.then_inc(sig_done, 1)
                if m >= 1:
                    act.wait_ge(ple_done, m)
                    for b in range(TB):
                        act.activation(junk[:, m - 1, b, :], hres[:, b, 512 * (m - 1):512 * m], ACT.Square,
                                       accum_out=sml[:, 32 + 4 * b + m - 1:33 + 4 * b + m - 1])
            act.wait_ge(ple_done, 4)
            for b in range(TB):
                act.activation(junk[:, 3, b, :], hres[:, b, 1536:2048], ACT.Square,
                               accum_out=sml[:, 35 + 4 * b:36 + 4 * b]).then_inc(ssq_done, 1)
            root(6, sml[:, 482:484])

        @block.tensor
        def _(pe):
            def wide(n, k, pair, x_of, first, last, loop=True):
                pe.wait_ge(lo_done, n + 1)
                for e in range(2):
                    xk = x_of(e)
                    for b in range(TB):
                        acc = bank[2 * pair + b][:]
                        wh, wl = hi[:, k, 512 * e:512 * e + 512], lo[:, k, 512 * e:512 * e + 512]
                        xh, xl = xk[:, 0, P * b:P * b + P], xk[:, 1, P * b:P * b + P]
                        pe.matmul(acc, xh, wh, start=first and e == 0, stop=False)
                        pe.matmul(acc, xh, wl, start=False, stop=False)
                        ins = pe.matmul(acc, xl, wh, start=False, stop=last and e == 1)
                ins.then_inc(unit_used, 1)

            def tall(n, k, acc, half):
                pe.wait_ge(lo_done, n + 1)
                for e in range(8):
                    xk = xop[:, 8 * half + e]
                    wh, wl = hi[:, k, P * e:P * e + P], lo[:, k, P * e:P * e + P]
                    pe.matmul(acc, wh, xk[:, 0, :], start=half == 0 and e == 0, stop=False)
                    pe.matmul(acc, wh, xk[:, 1, :], start=False, stop=False)
                    ins = pe.matmul(acc, wl, xk[:, 0, :], start=False, stop=half == 1 and e == 7)
                ins.then_inc(unit_used, 1)

            def chunk(m, n0, units, x_of, loop=False, pair=None, bias=False, weights=None):
                pair = m % 2 if pair is None else pair
                if bias and m >= M_PLE + 2:
                    pe.wait_ge(sig_done, m - M_PLE - 1)
                elif loop or m >= 2:
                    pe.wait_ge(mm_free, m - 1)
                for b in range(TB if bias else 0):
                    pe.matmul(bank[2 * pair + b][:], ones[0:1, :], brow[:, 512 * (m - M_PLE):512 * (m - M_PLE) + 512],
                              start=True, stop=False)
                for u in range(units):
                    if weights is not None:
                        pe.wait_ge(wexp_done, weights + u + 1)
                    wide(n0 + u, ((n0 if isinstance(n0, int) else 0) + u) % CV, pair, lambda e, u=u: x_of(2 * u + e),
                         u == 0 and not bias, u == units - 1)

            def turn(n):
                pe.wait_ge(xs_done, 2 * n + 2)
                for kk in range(KC // 2):
                    if kk >= 4:
                        pe.wait_ge(xt_gain, 16 * n + 2 * kk - 6)
                    for e in range(2):
                        for b in range(TB):
                            k = 2 * kk + e
                            ins = pe.transpose(bank[4 + kk % 4][:, S * e + P * b:S * e + P * b + P],
                                               xs[:, b, P * k:P * k + P], idn[:])
                    ins.then_inc(xt_ready, 1)

            pe.wait_ge(const_in, 16 * N_CONST)
            turn(0)
            pe.wait_ge(xt_split, 8)
            chunk(0, 0, 8, lambda k: xop[:, k])
            chunk(1, 8, 8, lambda k: xop[:, k])
            with pe.Fori(1, 3) as i:
                for e in range(2):
                    chunk(2 * i + e, 16 * i + 8 * e, 8, lambda k: xop[:, k], True, e)

            def side_tile(j):
                if j >= 2:
                    pe.wait_ge(st_free, j - 1)
                else:
                    pe.wait_ge(mm_free, 5)
                for u in range(2):
                    tall(U_XR + 2 * j + u, (2 * j + u) % CV, bank[j % 2][:, 0:S], u)

            for i in range(HEADS + 3):
                h = i
                if h < HEADS:
                    if h == 0:
                        pe.wait_ge(rope_done, 1)
                        pe.wait_ge(mm_free, 6)
                    else:
                        pe.wait_ge(ht_copied, h)
                    for q in range(2):
                        for b in range(TB):
                            ins = pe.transpose(bank[4][:, S * q + P * b:S * q + P * b + P],
                                               qk[:, b, A * q + P * h:A * q + P * h + P], idn[:])
                    ins.then_inc(ht_ready, 1)
                    side_tile(2 * i)
                h = i - 1
                if 0 <= h < HEADS:
                    pe.wait_ge(ht_copied, h + 1)
                    if h >= 1:
                        pe.wait_ge(sc_read, h)
                    qh, kh = qkt[:, h % 2, 0, :], qkt[:, h % 2, 1, :]
                    pe.matmul(bank[5][:, 0:P], qh[:, 0:P], kh[:, 0:P], start=True, stop=True)
                    pe.matmul(bank[5][:, P:384], qh[:, P:S], kh, start=True, stop=True).then_inc(sc_ready, 1)
                h = i - 2
                if 0 <= h < HEADS:
                    pe.wait_ge(prob_done, h + 1)
                    if h >= 1:
                        pe.wait_ge(pt_copied, h)
                    for j in range(3):
                        ins = pe.transpose(bank[6][:, P * j:P * j + P], sm[:, h % 2, P * j:P * j + P], idn[:])
                    ins.then_inc(pt_ready, 1)
                h = i - 3
                if 0 <= h < HEADS:
                    pe.wait_ge(pt_copied, h + 1)
                    if h >= 1:
                        pe.wait_ge(pv_gain, h)
                    v0, v1 = (vsb[:, b, P * h:P * h + P] for b in range(TB))
                    pr = pt[:, h % 2, :]
                    pe.matmul(bank[7][:, 0:P], v0, pr[:, 0:P], start=True, stop=True)
                    pe.matmul(bank[7][:, P:S], v0, pr[:, P:S], start=True, stop=False)
                    pe.matmul(bank[7][:, P:S], v1, pr[:, S:384], start=False, stop=True).then_inc(pv_ready, 1)
                if i < HEADS:
                    side_tile(2 * i + 1)
            pe.wait_ge(asum_ready, 1)
            for b in range(TB):
                ins = pe.matmul(bank[7][:, 256 + 2 * b:257 + 2 * b], sqsum[:, P * b:P * b + P], ones[:, 0:1],
                                start=True, stop=True)
            ins.then_inc(asum_out, 1)
            pe.wait_ge(st_free, 16)
            for m in range(2):
                chunk(M_OUTA + m, U_OUTA + 4 * m, 4, lambda k: atop[:, k])
            pe.wait_ge(bd_in, 64)
            pe.wait_ge(conv_done, 1)
            for n in range(2 * RC):
                if n >= 4:
                    pe.wait_ge(gates_done, n - 3)
                pe.matmul(bank[4 + n % 4][:, 0:S], bd[:, n // RC, n % RC, :], xc[:, n % RC, :],
                          start=True, stop=True).then_inc(bd_ready, 1)
            for m in range(2, 4):
                chunk(M_OUTA + m, U_OUTA + 4 * m, 4, lambda k: atop[:, k])
            pe.wait_ge(rm_gain, RC + 1)
            sq = naive.rearrange("p (c t) -> p c t", c=RC)
            for b in range(TB):
                for c in range(RC):
                    ins = pe.matmul(bank[7][:, 256 + 2 * b:257 + 2 * b], sq[:, c, P * b:P * b + P], ones[:, 0:1],
                                    start=c == 0, stop=c == RC - 1)
            ins.then_inc(rsum_out, 1)
            pe.wait_ge(rnn_split, 1)
            for m in range(4):
                chunk(M_OUTR + m, U_OUTR + 4 * m, 4, lambda k: xop[:, k])
            turn(1)
            pe.wait_ge(xt_split, 16)
            pe.wait_ge(sk_in, 16)

            def key_scores(j):
                pe.wait_ge(st_free, 16 + j + 1)
                if j >= 2:
                    pe.wait_ge(key_read, j - 1)
                for b in range(TB):
                    ins = pe.matmul(bank[6 + j % 2][:, P * b:P * b + P], qt[:, j % 2, P * b:P * b + P],
                                    skey[:, j, :], start=True, stop=True)
                ins.then_inc(key_ready, 1)

            for j in range(HC):
                if j >= 2:
                    pe.wait_ge(st_free, 16 + j - 1)
                for u in range(2):
                    tall(U_WQ + 2 * j + u, (2 * j + u) % CV, bank[j % 2][:, 0:S], u)
                if j >= 1:
                    key_scores(j - 1)
            key_scores(HC - 1)

            def expert_pair(n0, t, each=None):
                for b in range(2):
                    if not isinstance(t, int) or t + b >= 2:
                        pe.wait_ge(ua_free, t + b - 1)
                    for u in range(2):
                        tall(n0 + 2 * b + u, 2 * b + u, bank[4 + b][:, 0:S], u)
                    if each:
                        each(b)

            def spread(c, first):
                for s in range(4):
                    if s % 2 == 0:
                        pe.wait_ge(hot_done, 2 * c + s // 2 + 1)
                    if not first:
                        pe.wait_ge(g_copied, 4 * c + s - 3)
                    for k in range(4):
                        rows = hot[:, s // 2, :, :, 4 * (s % 2) + k]
                        for part in range(3):
                            ins = pe.matmul(bank[s][:, P * k:P * k + P], rows[:, 0], rows[:, 1 + part],
                                            start=part == 0, stop=part == 2)
                    ins.then_inc(g_ready, 1)

            expert_pair(U_U0, 0)
            with pe.Fori(1, GE) as i:
                expert_pair(U_U0 + 4 * i, 2 * i)
            for b in range(TB):
                pe.wait_ge(picked, b + 1)
                for q in range(3):
                    ins = pe.transpose(bank[6 + b][:, P * q:P * q + P], pick[:, b, q, :], idn[:])
                ins.then_inc(sel_ready, 1)
            expert_pair(U_U0 + 4 * GE, 2 * GE, lambda b: spread(b, b == 0))
            with pe.Fori(1, GE) as i:
                expert_pair(U_U0 + 4 * GE + 4 * i, 2 * GE + 2 * i, lambda b: spread(2 * i + b, False))
            with pe.Fori(0, GE // 2) as i:
                expert_pair(U_U0 + 8 * GE + 4 * i, 4 * GE + 2 * i)
            pe.wait_ge(g_copied, 64)

            def values(g, n0):
                with pe.Fori(0, 2) as q:
                    for e in range(2):
                        chunk(M_V + 4 * g + 2 * q + e, n0 + 8 * q + 4 * e, 4, lambda k: wop[:, k], True, e,
                              weights=4 * g)

            with pe.Fori(0, NG - AHEAD) as g:
                values(g, U_VU + 32 * g)
                with pe.Fori(0, GE // 2) as q:
                    expert_pair(U_VU + 32 * g + 16 + 4 * q, GE * (g + AHEAD) + 2 * q)
            with pe.Fori(NG - AHEAD, NG) as g:
                values(g, U_V1 + 16 * (g - (NG - AHEAD)))

            for m in range(4):
                chunk(M_PROJ + m, U_PROJ + m, 1, lambda k: pop[:, k])
            turn(2)
            pe.wait_ge(xt_split, 24)
            pe.wait_ge(late_in, 32)
            for m in range(4):
                chunk(M_PLE + m, U_PLE + 8 * m, 8, lambda k: xop[:, k], bias=True)

        @block.vector
        def _(dve):
            steps, issued = [0], [0]

            def link(ins):
                steps[0] = steps[0] + 1
                issued[0] += 1
                ins.then_inc(dve_step, 1)
                dve.wait_ge(dve_step, steps[0])

            def ts(out_, in_, s1, s2, op0, op1=ALU.bypass):
                return dve.tensor_scalar(out_, in_, s1, s2, op0, op1)

            def tt(out_, a_, b_, op):
                return dve.tensor_tensor(out_, a_, b_, op)

            def stt(out_, a_, s_, b_, op0, op1, **kw):
                return dve.scalar_tensor_tensor(out_, a_, s_, b_, op0, op1, **kw)

            def rstd(n, dst, src, width):
                ts(dst, src, 1.0 / width, EPS, ALU.mult, ALU.add).then_inc(mean_done, 1)
                dve.wait_ge(root_done, n + 1)
                link(dve.reciprocal(dst, dst))

            dve.wait_ge(const_in, 16 * N_CONST)
            link(ts(sml[:, 280:288], col[:, C_LAM:C_LAM + RC], -1.0, None, ALU.mult))
            link(tt(sml[:, 264:272], col[:, C_LAM:C_LAM + RC], sml[:, 280:288], ALU.max))
            ts(sml[:, 280:288], sml[:, 280:288], 0.0, None, ALU.max).then_inc(lam_done, 1)

            def scale_rows(n):
                dve.wait_ge(ssq_done, 2 * n + 2)
                rstd((0, 4, 5)[n], sml[:, 8 + 2 * n:10 + 2 * n], sml[:, 2 * n:2 * n + 2], D)
                for b in range(TB):
                    ts(xs[:, b, :], hres[:, b, :], sml[:, 8 + 2 * n + b:9 + 2 * n + b], None,
                       ALU.mult).then_inc(xs_done, 1)

            def split_operand(n):
                for kk in range(KC // 2):
                    dve.wait_ge(xt_gain, 16 * n + 2 * kk + 2)
                    src = tmp[:, kk % 2]
                    link(dve.tensor_copy(xop[:, 2 * kk:2 * kk + 2, 0, :], src))
                    tt(xop[:, 2 * kk:2 * kk + 2, 1, :], src, xop[:, 2 * kk:2 * kk + 2, 0, :].bitcast(F32),
                       ALU.subtract).then_inc(xt_split, 1)

            scale_rows(0)
            dve.wait_ge(rate_exp, 1)
            e_, z_, z2, pz = (sml[:, o:o + 8] for o in (272, 288, 296, 304))
            link(ts(z_, e_, 2.0, None, ALU.add))
            link(dve.reciprocal(z2, z_))
            link(tt(z_, e_, z2, ALU.mult))
            link(tt(z2, z_, z_, ALU.mult))
            link(ts(pz, z2, 1.0 / 17, 1.0 / 15, ALU.mult, ALU.add))
            for k in (13, 11, 9, 7, 5, 3, 1):
                link(tt(pz, pz, z2, ALU.mult))
                link(ts(pz, pz, 1.0 / k, None, ALU.add))
            link(tt(pz, pz, z_, ALU.mult))
            link(stt(pz, pz, 2.0, sml[:, 280:288], ALU.mult, ALU.add))
            rate = sml[:, 256:264]
            link(ts(rate, pz, RGLRU_C, None, ALU.mult))
            split_operand(0)
            ang, arg, trn = sml[:, 64:128], sml[:, 192:256], sml[:, 320:384]
            link(dve.tensor_copy(sml[:, 20:22], posi[:]))
            for b in range(TB):
                link(ts(arg[:, ROT * b:ROT * b + ROT], col[:, C_FREQ:C_FREQ + ROT], sml[:, 20 + b:21 + b], None, ALU.mult))
            link(dve.tensor_copy(arg[:, 32:64], arg[:, 0:32]))
            link(ts(trn[:, 0:32], arg[:, 0:32], 1.0 / TAU, None, ALU.mult))
            link(ts(trn[:, 32:64], arg[:, 32:64], 1.0 / TAU, 0.25, ALU.mult, ALU.add))
            link(ts(trn, trn, ROUND, None, ALU.add))
            link(ts(trn, trn, ROUND, None, ALU.subtract))
            link(stt(ang, trn, -TAU1, arg, ALU.mult, ALU.add))
            link(stt(ang, trn, -TAU2, ang, ALU.mult, ALU.add))
            link(stt(ang, trn, -TAU3, ang, ALU.mult, ALU.add))
            link(ts(ang[:, 32:64], ang[:, 32:64], TAU / 4, None, ALU.add))
            ts(ang, ang, 3.1415925, -3.1415925, ALU.min, ALU.max).then_inc(trig_ready, 1)
            link(dve.tensor_copy(pop[:, :, 0, :], praw))
            tt(pop[:, :, 1, :], praw, pop[:, :, 0, :].bitcast(F32), ALU.subtract).then_inc(pop_done, 1)
            dve.wait_ge(mm_free, 4)
            dve.wait_ge(sin_done, 1)
            for b in range(TB):
                rows = qk[:, b, :].rearrange("p (h d) -> p h d", d=P)
                x1, x2 = rows[:, :, 0:ROT], rows[:, :, ROT:2 * ROT]
                sn = sml[:, 128 + ROT * b:144 + ROT * b].unsqueeze(1).to_broadcast([P, 16, ROT])
                cs = sml[:, 160 + ROT * b:176 + ROT * b].unsqueeze(1).to_broadcast([P, 16, ROT])
                t1, t2 = (tmp[:, b, e].rearrange("p (h d) -> p h d", d=ROT) for e in range(2))
                tt(t1, x1, sn, ALU.mult)
                link(tt(t2, x2, sn, ALU.mult))
                tt(x1, x1, cs, ALU.mult)
                link(tt(x2, x2, cs, ALU.mult))
                tt(x1, x1, t2, ALU.subtract)
                link(tt(x2, x2, t1, ALU.add))
            dve.sem_inc(rope_done, 1)

            for i in range(HEADS + 3):
                h = i
                if h < HEADS:
                    dve.wait_ge(ht_ready, h + 1)
                    if h >= 2:
                        dve.wait_ge(sc_ready, h - 1)
                    dve.tensor_copy(ar[:, 6144 + 512 * (h % 2):6656 + 512 * (h % 2)], bank[4][:]).then_inc(ht_copied, 1)
                h = i - 1
                if 0 <= h < HEADS:
                    dve.wait_ge(sc_ready, h + 1)
                    if h >= 2:
                        dve.wait_ge(pt_ready, h - 1)
                    s_, st = sm[:, h % 2, :], 2 * (h % 2)
                    ins = tt(s_, bank[5][:, 0:384], madd, ALU.add)
                    ins.then_inc(sc_read, 1)
                    dve.wait_ge(sc_read, h + 1)
                    dve.tensor_reduce(sml[:, 400 + st:401 + st], s_[:, 0:P], AX_X, ALU.max)
                    link(dve.tensor_reduce(sml[:, 401 + st:402 + st], s_[:, P:384], AX_X, ALU.max))
                    ts(sml[:, 16 + st:18 + st], sml[:, 400 + st:402 + st], -SCALE, None, ALU.mult).then_inc(nmx_done, 1)
                    dve.wait_ge(exp_done, h + 1)
                    stt(s_[:, 0:P], s_[:, 0:P], 1.0, mcnt[:, 0:P], ALU.mult, ALU.mult, accum_out=sml[:, 404 + st:405 + st])
                    link(stt(s_[:, P:384], s_[:, P:384], 1.0, mcnt[:, P:384], ALU.mult, ALU.mult,
                             accum_out=sml[:, 405 + st:406 + st]))
                    link(dve.reciprocal(sml[:, 408 + st:410 + st], sml[:, 404 + st:406 + st]))
                    ts(s_[:, 0:P], s_[:, 0:P], sml[:, 408 + st:409 + st], None, ALU.mult)
                    ts(s_[:, P:384], s_[:, P:384], sml[:, 409 + st:410 + st], None, ALU.mult).then_inc(prob_done, 1)
                h = i - 3
                if 0 <= h < HEADS:
                    dve.wait_ge(pv_gain, h + 1)
                    if h == 0:
                        link(dve.tensor_copy(sqsum, sqt[:, 0, :]))
                    else:
                        link(tt(sqsum, sqsum, sqt[:, h % 2, :], ALU.add))
                    link(dve.tensor_copy(atop[:, h, 0, :], at[:, h % 2, :]))
                    tt(atop[:, h, 1, :], at[:, h % 2, :], atop[:, h, 0, :].bitcast(F32), ALU.subtract).then_inc(at_split, 1)
            dve.sem_inc(asum_ready, 1)
            dve.wait_ge(pv_ready, HEADS)
            dve.memset(ar[:, 4096:6144], 0.0).then_inc(bd_zero, 1)
            dve.wait_ge(st_free, RC)
            for c in range(RC):
                ins = ts(xc[:, c, :], xr[:, c, :], col[:, C_CW + 3 * RC + c:C_CW + 3 * RC + c + 1],
                         col[:, C_CB + c:C_CB + c + 1], ALU.mult, ALU.add)
            link(ins)
            for k in range(TAPS - 1):
                lag = TAPS - 1 - k
                for c in range(RC):
                    ins = stt(xc[:, c, lag:S], xr[:, c, 0:S - lag], col[:, C_CW + k * RC + c:C_CW + k * RC + c + 1],
                              xc[:, c, lag:S], ALU.mult, ALU.add)
                if k == TAPS - 2:
                    ins.then_inc(conv_done, 1)
                else:
                    link(ins)
            dve.wait_ge(asum_out, 1)
            rstd_a, rstd_r = sml[:, 24:26], sml[:, 26:28]
            sums = bank[7][:, 256:260].rearrange("p (b e) -> p b e", e=2)[:, :, 0]
            rstd(1, rstd_a, sums, A)

            def add_mixed(m, end, r):
                dve.wait_ge(unit_used, end)
                o = 512 * ((m - M_OUTA) % 4)
                for b in range(TB):
                    ins = stt(hres[:, b, o:o + 512], bank[m % 2 * 2 + b][:], r[:, b:b + 1], hres[:, b, o:o + 512],
                              ALU.mult, ALU.add)
                ins.then_inc(mm_free, 1)

            add_mixed(M_OUTA, U_OUTA + 4, rstd_a)
            add_mixed(M_OUTA + 1, U_OUTA + 8, rstd_a)
            dve.wait_ge(gates_done, 2 * RC)
            lw, aw, iw, xw = ar[:, 2048:4096], ar[:, 8192:10240], ar[:, 6144:8192], ar[:, 0:2048]
            tt(rg, rg, rate.unsqueeze(2).to_broadcast([P, RC, S]), ALU.mult).then_inc(l_done, 1)
            dve.wait_ge(l_done, 1)
            link(tt(iw, iw, xw, ALU.mult))
            yw = xw
            link(ts(yw, lw, 2.0, 0.25, ALU.mult, ALU.min))
            link(ts(poly, yw, -1.0 / 720, None, ALU.mult))
            for f in (1.0 / 120, -1.0 / 24, 1.0 / 6, -0.5, 1.0):
                link(stt(poly, poly, f, yw, ALU.add, ALU.mult))
            add_mixed(M_OUTA + 2, U_OUTA + 12, rstd_a)
            dve.wait_ge(a_done, 1)
            link(tt(naive, aw, aw, ALU.mult))
            link(ts(naive, naive, -1.0, 1.0, ALU.mult, ALU.add))
            link(ts(yw, yw, 0.25, None, ALU.is_lt))
            dve.copy_predicated(naive, yw.bitcast(U32), poly).then_inc(mean_done, 1)
            add_mixed(M_OUTA + 3, U_OUTA + 16, rstd_a)
            dve.wait_ge(root_done, 3)
            link(tt(iw, iw, naive, ALU.mult))
            for c in range(RC):
                ins = dve.tensor_tensor_scan(rg[:, c, :], av[:, c, :], ig[:, c, :], 0.0, ALU.mult, ALU.add)
            link(ins)
            dve.wait_ge(gelu_done, 1)
            tt(ar[:, 12288:14336], lw, ar[:, 12288:14336], ALU.mult).then_inc(rm_done, 1)
            dve.wait_ge(rm_gain, RC)
            for k in range(2):
                link(dve.tensor_copy(xop[:, 4 * k:4 * k + 4, 0, :], ig[:, 4 * k:4 * k + 4, :]))
                ins = tt(xop[:, 4 * k:4 * k + 4, 1, :], ig[:, 4 * k:4 * k + 4, :],
                         xop[:, 4 * k:4 * k + 4, 0, :].bitcast(F32), ALU.subtract)
            ins.then_inc(rnn_split, 1)
            dve.wait_ge(rsum_out, 1)
            rstd(3, rstd_r, sums, A)
            for m in range(4):
                add_mixed(M_OUTR + m, U_OUTR + 4 * m + 4, rstd_r)
            scale_rows(1)
            split_operand(1)

            def top16(vals, work, last):
                for v, w_, t, ix in vals:
                    ins = dve.max(t[:, 0:8], v)
                link(ins)
                for v, w_, t, ix in vals:
                    dve.max_index(ix[:, 0:8], t[:, 0:8], v)
                for v, w_, t, ix in vals:
                    ins = dve.match_replace(w_, t[:, 0:8], v, NEG)
                if last is not None:
                    ins.then_inc(last, 1)
                    dve.wait_ge(last, last_at[0])
                else:
                    link(ins)
                for v, w_, t, ix in vals:
                    ins = dve.max(t[:, 8:16], w_)
                link(ins)
                for v, w_, t, ix in vals:
                    ins = dve.max_index(ix[:, 8:16], t[:, 8:16], w_)
                return ins

            last_at = [0]
            for j in range(HC):
                dve.wait_ge(key_ready, j + 1)
                last_at[0] = j + 1
                ins = top16([(bank[6 + j % 2][:, P * b:P * b + P], tkw[:, b, 0:P], tks[:, b, j, :], tki[:, b, j, :])
                             for b in range(TB)], None, key_read)
            link(ins)
            link(dve.tensor_copy(ar[:, 9216:9728], ar[:, 8704:9216].bitcast(U32)))

            for b in range(TB):
                s2 = tks[:, b].rearrange("p (h c) k -> p h c k", c=2)
                i2 = tkf[:, b].rearrange("p (h c) k -> p h c k", c=2)
                link(tt(cand, s2[:, :, 0, :].unsqueeze(3).to_broadcast([P, PH, TOPK, TOPK]),
                        s2[:, :, 1, :].unsqueeze(2).to_broadcast([P, PH, TOPK, TOPK]), ALU.add))
                pb = pos[:, b, :].rearrange("p (h k) -> p h k", k=TOPK)
                for hp in range(PH // 2):
                    ins = top16([(cand[:, h].rearrange("p a b -> p (a b)"), tkw[:, h % 2, :], best[:, b, h, :], pb[:, h, :])
                                 for h in (2 * hp, 2 * hp + 1)], None, None)
                    if hp < PH // 2 - 1:
                        link(ins)
                exb = ex[:, b, :].rearrange("p (h k) -> p h k", k=TOPK)
                link(ins)
                tt(exb, best[:, b], best[:, b, :, 0:1].to_broadcast([P, PH, TOPK]), ALU.subtract).then_inc(bm_done, 1)
                qd = tmp[:, 1, :, 0:P]
                link(ts(eq[:, 0:1].rearrange("p n a b -> p (n a b)")[:, 0:P].bitcast(U32), pos[:, b, :], 4, None,
                        ALU.logical_shift_right))
                link(dve.tensor_copy(qd[:, 0, :], eq[:, 0:1].rearrange("p n a b -> p (n a b)")[:, 0:P].bitcast(U32)))
                link(ts(eq[:, 0:1].rearrange("p n a b -> p (n a b)")[:, 0:P].bitcast(U32), pos[:, b, :], 15, None,
                        ALU.bitwise_and))
                link(dve.tensor_copy(qd[:, 1, :], eq[:, 0:1].rearrange("p n a b -> p (n a b)")[:, 0:P].bitcast(U32)))
                for q in range(2):
                    flat = eq.rearrange("p n a b -> p (n a) b")
                    link(tt(flat, qd[:, q, :].unsqueeze(2).to_broadcast([P, P, TOPK]),
                            iot[:, 0:TOPK].unsqueeze(1).to_broadcast([P, P, TOPK]), ALU.is_equal))
                    link(tt(eq, eq, i2[:, :, q, :].unsqueeze(2).to_broadcast([P, PH, TOPK, TOPK]), ALU.mult))
                    link(dve.tensor_reduce(pick[:, b, q, :], flat, AX_X, ALU.add))
            dve.wait_ge(eg_done, 1)
            for b in range(TB):
                exb = ex[:, b, :].rearrange("p (h k) -> p h k", k=TOPK)
                link(dve.tensor_reduce(sml[:, 416:424], exb, AX_X, ALU.add))
                link(dve.reciprocal(sml[:, 424:432], sml[:, 416:424]))
                tt(pick[:, b, 2, :].rearrange("p (h k) -> p h k", k=TOPK), exb,
                   sml[:, 424:432].unsqueeze(2).to_broadcast([P, PH, TOPK]), ALU.mult).then_inc(picked, 1)
            dve.tensor_copy(irep, iot[:].unsqueeze(2).to_broadcast([P, P, 8]))
            for b in range(TB):
                dve.wait_ge(sel_ready, b + 1)
                dve.tensor_copy(keyb[:, :, P * b:P * b + P], bank[6 + b][:, 0:S].rearrange("p (q t) -> p q t", q=2))
                link(dve.tensor_copy(grest[:, P * b:P * b + P], bank[6 + b][:, S:384]))
            for part in range(3):
                link(dve.tensor_copy(gpart[:, part, :], grest[:]))
                if part < 2:
                    link(tt(grest[:], grest[:], gpart[:, part, :], ALU.subtract))

            def hot_rows(q, b):
                at_ = bass.ds(8 * q, 8) if not isinstance(q, int) else slice(8 * q, 8 * q + 8)
                if not isinstance(q, int) or q >= 2:
                    dve.wait_ge(g_ready, 2 * q - 2)

                def over(row):
                    return row.unsqueeze(1).to_broadcast([P, P, 8])

                tt(hot[:, b, 0], irep, over(keyb[:, 1, at_]), ALU.is_equal)
                link(tt(eqb[:, b], irep, over(keyb[:, 0, at_]), ALU.is_equal))
                for part in range(3):
                    ins = tt(hot[:, b, 1 + part], eqb[:, b], over(gpart[:, part, at_]), ALU.mult)
                ins.then_inc(hot_done, 1)

            for b in range(2):
                hot_rows(b, b)
            start = steps[0]
            with dve.Fori(1, S // 16) as i:
                steps[0] = start + 2 * (i - 1)
                for b in range(2):
                    hot_rows(2 * i + b, b)
            steps[0] = start + 2 * (S // 16 - 1)

            def weigh(g):
                dve.wait_ge(g_in, 16 * g + 16)
                a4 = ar[:, bass.ds(g % AHEAD * (GE * S), GE * S)].rearrange("p (j c t) -> p j c t", j=GE, t=16)
                tt(a4, a4, gt.rearrange("p (c j t) -> p j c t", j=GE, t=16), ALU.mult).then_inc(g_used, 1)

            def split_weights(g, n0):
                dve.wait_ge(g_used, g + 1)
                w3 = ar[:, bass.ds(g % AHEAD * (GE * S), GE * S)].rearrange("p (j t) -> p j t", t=S)
                for u in range(4):
                    if n0 is not None:
                        dve.wait_ge(unit_used, n0 + u + 1)
                    two = slice(2 * u, 2 * u + 2)
                    link(ts(wop[:, two, 0, :], w3[:, two, :], 1.0, None, ALU.mult))
                    tt(wop[:, two, 1, :], w3[:, two, :], wop[:, two, 0, :].bitcast(F32),
                       ALU.subtract).then_inc(wexp_done, 1)

            def add_values(n0, chunks):
                for c in chunks:
                    dve.wait_ge(unit_used, n0 + 4 * c + 4)
                    for b in range(TB):
                        ins = tt(hres[:, b, 512 * c:512 * c + 512], bank[c % 2 * 2 + b][:],
                                 hres[:, b, 512 * c:512 * c + 512], ALU.add)
                    ins.then_inc(mm_free, 1)

            dve.wait_ge(g_ready, 64)
            dve.wait_ge(ua_free, GE)
            weigh(0)
            split_weights(0, None)

            def between(g, n0, wait):
                add_values(n0, (0, 1))
                if wait:
                    dve.wait_ge(ua_free, GE * (g + 2))
                weigh(g + 1)
                add_values(n0, (2,))
                split_weights(g + 1, n0 + 12)
                add_values(n0, (3,))

            start = steps[0]
            with dve.Fori(0, NG - AHEAD) as g:
                steps[0] = start + 4 * g
                between(g, U_VU + 32 * g, True)
            start = start + 4 * (NG - AHEAD)
            with dve.Fori(NG - AHEAD, NG - 1) as g:
                steps[0] = start + 4 * (g - (NG - AHEAD))
                between(g, U_V1 + 16 * (g - (NG - AHEAD)), False)
            steps[0] = start + 4 * (AHEAD - 1)
            add_values(U_V1 + 16 * (AHEAD - 1), range(4))

            scale_rows(2)
            split_operand(2)
            for m in range(4):
                dve.wait_ge(sig_done, m + 1)
                for b in range(TB):
                    link(tt(sg[:, m % 2, b, :], sg[:, m % 2, b, :], pp[:, b, 512 * m:512 * m + 512], ALU.mult))
                    ins = tt(hres[:, b, 512 * m:512 * m + 512], hres[:, b, 512 * m:512 * m + 512], sg[:, m % 2, b, :],
                             ALU.add)
                ins.then_inc(ple_done, 1)
            dve.wait_ge(ssq_done, 8)
            dve.wait_ge(late_in, 32)
            link(dve.tensor_reduce(sml[:, 480:482], sml[:, 32:40].rearrange("p (b m) -> p b m", b=TB), AX_X, ALU.add))
            rstd(6, sml[:, 482:484], sml[:, 480:482], D)
            for b in range(TB):
                stt(xs[:, b, :], hres[:, b, :], sml[:, 482 + b:483 + b], fnb, ALU.mult, ALU.mult).then_inc(y_done, 1)


_OUT = (1, S, D)


def wide_units(w, n0, n1):
    k, n = w.shape
    t = w.reshape(k // 256, 2, P, n // 512, 512).transpose(3, 0, 2, 1, 4)
    return t.reshape(-1, P, UW)[n0:n1]


def tall_units(w):
    k, n = w.shape
    return w.reshape(k // 1024, 8, P, n // P, P).transpose(3, 0, 2, 1, 4).reshape(-1, P, UW)


def kernel(**inputs):
    import concourse.bacc as bacc
    from concourse.bass_utils import run_bass_kernel_spmd

    a = {n: np.asarray(v) for n, v in inputs.items()}
    w_in, w_out = a["w_in"][0], a["w_out"][0]
    u, v = a["peer_u"][0], a["peer_v"][0]
    u_groups = tall_units(u.T).reshape(NG, 16, P, UW)
    v_groups = (v.reshape(NG, 4, 2, P, 4, 512).transpose(0, 4, 1, 3, 2, 5).reshape(NG, 16, P, UW))
    parts = [wide_units(w_in[:, 0:3 * A], 0, 48), tall_units(w_in[:, 3 * A:]),
             wide_units(w_out[0:A], 0, 16), wide_units(w_out[A:], 0, 16), tall_units(a["peer_wq"][0])]
    parts += [u_groups[g] for g in range(AHEAD)]
    for g in range(NG - AHEAD):
        parts += [v_groups[g], u_groups[g + AHEAD]]
    parts += [v_groups[g] for g in range(NG - AHEAD, NG)]
    parts += [wide_units(a["ple_proj"][0], 0, 4), wide_units(a["ple_w_gate"][0], 0, 32)]
    stream = np.concatenate(parts)

    def by_channel(t):
        return t.reshape(-1, P).T

    half = np.arange(ROT, dtype=np.float32)
    freq = (np.float32(500000.0) ** (-half * np.float32(2.0) / np.float32(2 * ROT))).astype(np.float32)
    cols = np.concatenate([by_channel(a["mix_norm"][0]), by_channel(a["ffn_norm"][0]), by_channel(a["ple_norm"][0]),
                           by_channel(a["attn_out_norm"][0]), by_channel(a["rnn_out_norm"][0]),
                           by_channel(a["conv_w"][0]), by_channel(a["conv_b"][0]), by_channel(a["rg_ba"][0]),
                           by_channel(a["rg_bx"][0]), by_channel(a["rg_lambda"][0]),
                           np.broadcast_to(freq, (P, ROT))], axis=1)
    lag = np.arange(S)[:, None] - np.arange(S)[None, :]
    count = (lag >= 0) * ((lag <= 128) * 1.0 + (lag % 4 == 0) + (lag % 16 == 0))
    count = np.concatenate([count[0:P, 0:P], count[P:]], axis=1).astype(np.float32)
    masks = np.stack([np.where(count > 0, 0.0, MASKED).astype(np.float32), count])
    arrays = {
        "stream": stream, "x": a["x"][0], "positions": a["positions"][0].reshape(TB, P).T, "cols": cols, "masks": masks,
        "w_a": a["rg_wa"][0], "w_x": a["rg_wx"][0],
        "subkeys": a["peer_subkeys"][0].reshape(HC, KEYS, P).transpose(2, 0, 1).reshape(P, HC * KEYS),
        "p_t": a["p"][0, 0].T.reshape(2, P, S).transpose(1, 0, 2), "b_gate": a["ple_b_gate"],
        "final_norm": np.broadcast_to(a["final_norm"], (P, D)),
        "iota": np.broadcast_to(np.arange(P, dtype=np.float32), (P, P)), "ident": np.eye(P, dtype=np.float32),
    }
    arrays = {n: np.ascontiguousarray(t) for n, t in arrays.items()}
    nc = bacc.Bacc("TRN2", target_bir_lowering=False, num_devices=1)
    aps = {n: nc.dram_tensor(f"in_{n}", t.shape, mybir.dt.from_np(t.dtype), kind="ExternalInput").ap()
           for n, t in arrays.items()}
    g_dram = nc.dram_tensor("spread", (NG, P, 16 * P), F32, kind="Internal").ap()
    out = nc.dram_tensor("out", (S, D), F32, kind="ExternalOutput").ap()
    build(nc, **aps, g_dram=g_dram, out=out)
    r = run_bass_kernel_spmd(nc, [{f"in_{n}": t for n, t in arrays.items()}], core_ids=[0])
    return r.results[0]["out"].reshape(_OUT)
```

```python
from contextlib import ExitStack

import numpy as np
import concourse.bass as bass
from concourse import mybir

ALU = mybir.AluOpType
ACT = mybir.ActivationFunctionType
AX_X = mybir.AxisListType.X
F32 = mybir.dt.float32
BF16 = mybir.dt.bfloat16
F32R = mybir.dt.float32r
I32 = mybir.dt.int32
U32 = mybir.dt.uint32

P = 128
S = 256
TB = S // P
D = 2048
KC = D // P
HEADS = 8
A = HEADS * P
RC = 8
ROT = 16
SCALE = float(P) ** -0.5
EPS = 1e-6
TAPS = 4
RGLRU_C = 8.0
PH = 8
HC = 2 * PH
KEYS = 128
TOPK = 16
SLOTS = PH * TOPK
NEG = -3.0e38
MASKED = -1.0e30

UW = 1024
RAW = 8
CV = 4
GE = 8
NG = 128 // GE
AHEAD = 5
U_XR = 0
U_GATE = U_XR + 16
U_QKV = U_GATE + 16
U_OUTR = U_QKV + 48
U_OUTA = U_OUTR + 16
U_WQ = U_OUTA + 16
U_U0 = U_WQ + 32
U_VU = U_U0 + 16 * AHEAD
U_V1 = U_VU + 32 * (NG - AHEAD)
U_PROJ = U_V1 + 16 * AHEAD
U_PLE = U_PROJ + 4
UNITS = U_PLE + 32
M_OUTR, M_OUTA, M_V = 6, 10, 14
M_PROJ = M_V + 4 * NG
M_PLE = M_PROJ + 4
C_MIX, C_FFN, C_PLE = 0, 16, 32
C_GA, C_GR, C_CW, C_CB, C_BA, C_BX, C_LAM = 48, 56, 64, 96, 104, 112, 120
C_FREQ = 128
C_END = 144
TAU = 6.283185307179586
TAU1 = 6.28125
TAU2 = 0.0019350051879882812
TAU3 = 3.019915981956753e-07
ROUND = 12582912.0


def build(nc, stream, x, x_t, positions, cols, masks, w_a, w_x, subkeys, p_t, b_gate, final_norm, iota, ident, g_dram, out):
    ctx = ExitStack()
    with ctx:
        def sb(name, shape, dt=F32):
            return ctx.enter_context(nc.sbuf_tensor(name, shape, dt))

        def sem(name):
            return ctx.enter_context(nc.semaphore(name))

        bank = [ctx.enter_context(nc.psum_tensor(f"bank{i}", [P, 512], F32)) for i in range(8)]
        xop = sb("xop", [P, KC, 2, S], F32R)
        with nc.sbuf_tensor("rtmp", [P, 2, D], F32) as rtmp:
            pass
        with nc.sbuf_tensor("rop", [P, GE, 2, S], F32R) as rop:
            pass
        with nc.sbuf_tensor("hot", [P, 2, 4, P, 8], BF16) as hot:
            pass
        wop = sb("wop", [P, GE, 2, S], F32R)
        pop = sb("pop", [P, 2, 2, S], F32R)
        hi = sb("hi", [P, CV, UW], F32R)
        lo = sb("lo", [P, CV, UW], F32R)
        raw = sb("raw", [P, RAW, UW])
        hres = sb("hres", [P, TB, D])
        arena = sb("arena", [P, 14336])
        idn = sb("idn", [P, P])
        iot = sb("iot", [P, P])
        col = sb("col", [P, C_END])
        ones = sb("ones", [P, P])
        sml = sb("sml", [P, 512])
        posi = sb("posi", [P, TB], I32)
        tmp = sb("tmp", [P, 2, 2, S])
        pick = sb("pick", [P, 2, 3, P])
        pos = sb("pos", [P, 2, P], U32)
        keyb = sb("keyb", [P, 2, S], BF16)
        gpart = sb("gpart", [P, 3, S], BF16)
        bc = sb("bc", [P, S])
        grest = sb("grest", [P, S])

        sqt, sqsum = tmp[:, 0], tmp[:, 1, 0]
        qt, tkw = tmp[:, 0], tmp[:, 1]

        ar = arena
        xs = ar[:, 0:4096].rearrange("p (b d) -> p b d", b=TB)
        xtr = ar[:, 0:4096].rearrange("p (k t) -> p k t", k=KC)
        qk = xs
        vsb = ar[:, 4096:6144].rearrange("p (b d) -> p b d", b=TB)
        qkt = ar[:, 6144:7168].rearrange("p (n q t) -> p n q t", n=2, q=2)
        madd, mcnt = ar[:, 10240:10624], ar[:, 10624:11008]
        sm = ar[:, 7936:8704].rearrange("p (n k) -> p n k", n=2)
        pt = ar[:, 8704:9472].rearrange("p (n k) -> p n k", n=2)
        at = ar[:, 9472:9984].rearrange("p (n t) -> p n t", n=2)
        xr = ar[:, 10240:12288].rearrange("p (c t) -> p c t", c=RC)
        gate = ar[:, 12288:14336].rearrange("p (c t) -> p c t", c=RC)
        xc = rtmp[:, 0, :].rearrange("p (c t) -> p c t", c=RC)
        bd = rtmp[:, 1, :].rearrange("p (m c d) -> p m c d", m=2, c=RC)
        rg = ar[:, 4096:6144].rearrange("p (c t) -> p c t", c=RC)
        ig = ar[:, 6144:8192].rearrange("p (c t) -> p c t", c=RC)
        av = ar[:, 8192:10240].rearrange("p (c t) -> p c t", c=RC)
        poly = ar[:, 10240:12288]
        naive = rtmp[:, 1, :]
        rsq = ar[:, 8192:10240]
        skey = ar[:, 4096:6144].rearrange("p (n k) -> p n k", n=HC)
        tks = ar[:, 8192:8704].rearrange("p (b n k) -> p b n k", b=TB, n=HC)
        tki = ar[:, 8704:9216].bitcast(U32).rearrange("p (b n k) -> p b n k", b=TB, n=HC)
        tkf = ar[:, 9216:9728].rearrange("p (b n k) -> p b n k", b=TB, n=HC)
        best = ar[:, 9728:9984].rearrange("p (b n k) -> p b n k", b=TB, n=PH)
        ex = ar[:, 9984:10240].rearrange("p (b n) -> p b n", b=TB)
        cand = ar[:, 10240:12288].rearrange("p (n a b) -> p n a b", n=PH, a=TOPK)
        eq = ar[:, 12288:14336].rearrange("p (n a b) -> p n a b", n=PH, a=TOPK)
        stg = [ar[:, 8192:10240], ar[:, 12288:14336]]
        gt = ar[:, 10240:12288]
        irep = ar[:, 10240:10752].bitcast(BF16).rearrange("p (i t) -> p i t", t=8)
        eqb = ar[:, 10752:11776].bitcast(BF16).rearrange("p (n i t) -> p n i t", n=2, t=8)
        fnb = ar[:, 8192:10240]
        pp = ar[:, 4096:8192].rearrange("p (b d) -> p b d", b=TB)
        bias = ar[:, 10240:12288]
        xg = ar[:, 0:4096].rearrange("p (k t) -> p k t", k=KC)
        junks = [ar[:, o:o + 4096].rearrange("p (n b d) -> p n b d", n=4, b=TB) for o in (8192, 0)]
        sg = ar[:, 12288:14336].rearrange("p (n b d) -> p n b d", n=2, b=TB)
        praw = ar[:, 10240:10752].rearrange("p (c t) -> p c t", c=2)
        ring = AHEAD * GE * S

        raw_in = [sem(f"raw_in{i}") for i in range(RAW)]
        hi_done, lo_done, unit_used = sem("hi_done"), sem("lo_done"), sem("unit_used")
        const_in, x_in, bd_in, sk_in, late_in = sem("const_in"), sem("x_in"), sem("bd_in"), sem("sk_in"), sem("late_in")
        xt_in = [sem(f"xt_in{i}") for i in range(4)]
        mask_in, diag_done, bc_ready, bc_copied = sem("mask_in"), sem("diag_done"), sem("bc_ready"), sem("bc_copied")
        xg_scaled, xg_high = sem("xg_scaled"), sem("xg_high")
        mm_free, st_free, ua_free = sem("mm_free"), sem("st_free"), sem("ua_free")
        ssq_done = sem("ssq_done")
        xt_ready, xt_gain, xt_split = sem("xt_ready"), sem("xt_gain"), sem("xt_split")
        dve_step = sem("dve_step")
        trig_ready, sin_done = sem("trig_ready"), sem("sin_done")
        rope_done = sem("rope_done")
        ht_ready, ht_copied = sem("ht_ready"), sem("ht_copied")
        sc_ready, sc_read = sem("sc_ready"), sem("sc_read")
        nmx_done, exp_done, prob_done = sem("nmx_done"), sem("exp_done"), sem("prob_done")
        pt_ready, pt_copied = sem("pt_ready"), sem("pt_copied")
        pv_ready, pv_gain, at_split = sem("pv_ready"), sem("pv_gain"), sem("at_split")
        asum_ready, asum_out = sem("asum_ready"), sem("asum_out")
        bd_zero, conv_done, bd_ready = sem("bd_zero"), sem("conv_done"), sem("bd_ready")
        gates_done, l_done, a_done = sem("gates_done"), sem("l_done"), sem("a_done")
        rnn_split, rsum_ready, rsum_out = sem("rnn_split"), sem("rsum_ready"), sem("rsum_out")
        key_ready, key_read = sem("key_ready"), sem("key_read")
        bm_done, eg_done, picked = sem("bm_done"), sem("eg_done"), sem("picked")
        sel_ready, sel_read = sem("sel_ready"), sem("sel_read")
        hot_done, g_ready, g_copied = sem("hot_done"), sem("g_ready"), sem("g_copied")
        g_out = [sem("g_out0"), sem("g_out1")]
        g_in, g_used, wexp_done = sem("g_in"), sem("g_used"), sem("wexp_done")
        sig_done, ple_done, y_done, out_done = sem("sig_done"), sem("ple_done"), sem("y_done"), sem("out_done")
        mean_done, root_done = sem("mean_done"), sem("root_done")
        one_done, pop_done, lam_done, gelu_done = sem("one_done"), sem("pop_done"), sem("lam_done"), sem("gelu_done")
        rate_exp, rm_done, rm_gain, pj_done = sem("rate_exp"), sem("rm_done"), sem("rm_gain"), sem("pj_done")

        N_CONST = 5

        block = ctx.enter_context(nc.Block())

        @block.sync
        def _(sp):
            for b in range(RAW):
                if b < 4:
                    sp.dma_start(xtr[:, 4 * b:4 * b + 4, :], x_t[:, 4 * b:4 * b + 4, :]).then_inc(xt_in[b], 16)
                sp.dma_start(raw[:, b, :], stream[b]).then_inc(raw_in[b], 16)
            with sp.Fori(1, UNITS // RAW) as i:
                for b in range(RAW):
                    sp.wait_ge(lo_done, RAW * i + b - RAW + 1)
                    sp.dma_start(raw[:, b, :], stream[RAW * i + b]).then_inc(raw_in[b], 16)
            for n in range(UNITS // RAW * RAW, UNITS):
                sp.wait_ge(lo_done, n - RAW + 1)
                sp.dma_start(raw[:, n % RAW, :], stream[n]).then_inc(raw_in[n % RAW], 16)
            for b in range(TB):
                for e in range(2):
                    sp.wait_ge(y_done, 2 * b + e + 1)
                    sp.dma_start(out[P * b:P * b + P, 1024 * e:1024 * e + 1024],
                                 xs[:, b, 1024 * e:1024 * e + 1024]).then_inc(out_done, 16)
            sp.wait_ge(out_done, 64)

        @block.gpsimd
        def _(pool):
            pool.memset(ones[:], 1.0).then_inc(one_done, 1)
            with pool.Fori(0, UNITS // CV // 2) as i:
                for b in range(2 * CV):
                    pool.wait_ge(hi_done, 2 * CV * i + b + 1)
                    pool.tensor_tensor(lo[:, b % CV, :], raw[:, b, :], hi[:, b % CV, :].bitcast(F32),
                                       ALU.subtract).then_inc(lo_done, 1)
            for n in range(UNITS // (2 * CV) * 2 * CV, UNITS):
                pool.wait_ge(hi_done, n + 1)
                pool.tensor_tensor(lo[:, n % CV, :], raw[:, n % RAW, :], hi[:, n % CV, :].bitcast(F32),
                                   ALU.subtract).then_inc(lo_done, 1)

        @block.scalar
        def _(act):
            made = [0]

            def round_unit(n, k, loop):
                act.wait_ge(raw_in[k], 2 * (n - k) + 16)
                if loop or n >= CV:
                    act.wait_ge(unit_used, n - CV + 1)
                act.activation(hi[:, k % CV, :], raw[:, k, :], ACT.Copy).then_inc(hi_done, 1)

            def round_to(n):
                while made[0] <= min(n, UNITS - 1):
                    round_unit(made[0], made[0] % RAW, False)
                    made[0] += 1

            act.dma_start(col[:], cols).then_inc(const_in, 16)
            act.dma_start(hres[:, 0, :], x[0:P, :]).then_inc(x_in, 16)
            act.dma_start(hres[:, 1, :], x[P:S, :]).then_inc(x_in, 16)
            act.dma_start(praw, p_t).then_inc(const_in, 16)
            act.dma_start(idn[:], ident).then_inc(const_in, 16)
            act.dma_start(posi[:], positions).then_inc(const_in, 16)
            act.dma_start(iot[:], iota).then_inc(const_in, 16)

            def root(n, at_):
                act.wait_ge(mean_done, n + 1)
                act.activation(at_, at_, ACT.Sqrt).then_inc(root_done, 1)

            def squares(n, m, c):
                act.wait_ge(mm_free, m + 1)
                for b in range(TB):
                    ins = act.activation(junks[n - 1][:, c, b, :], hres[:, b, 512 * c:512 * c + 512], ACT.Square,
                                         accum_out=sml[:, 32 + 4 * b + c:33 + 4 * b + c])
                ins.then_inc(ssq_done, 1)

            def gains(n, c0, ks, src):
                for k in ks:
                    if k % 2 == 0 and n:
                        act.wait_ge(xt_ready, 8 * (n - 1) + k // 2 + 1)
                    if k % 2 == 0 and n != 1 and k >= 4:
                        act.wait_ge(xt_split, 8 * n + k // 2 - 1)
                    act.activation(xg[:, k, :] if n == 1 else tmp[:, k // 2 % 2, k % 2, :], src(k), ACT.Copy,
                                   scale=col[:, c0 + k:c0 + k + 1]).then_inc(xt_gain, 1)

            def turned(k):
                return bank[4 + k // 2 % 4][:, k % 2 * S:k % 2 * S + S]

            act.wait_ge(const_in, 16 * N_CONST)
            for u in range(4):
                act.wait_ge(xt_in[u], 16)
                gains(0, C_MIX, range(4 * u, 4 * u + 4), lambda k: xtr[:, k, :])
                round_to(u)
            act.wait_ge(bd_zero, 1)
            for m, w in enumerate((w_a, w_x)):
                for e in range(2):
                    act.dma_start(bd[64 * e:64 * e + 64, m, :, 64 * e:64 * e + 64],
                                  w.rearrange("(c e) i o -> e i c o", e=2)[e]).then_inc(bd_in, 16)
            act.wait_ge(x_in, 32)
            for b in range(TB):
                act.wait_ge(xt_gain, KC)
                act.activation(xs[:, b, :], hres[:, b, :], ACT.Square,
                               accum_out=sml[:, b:b + 1]).then_inc(ssq_done, 1)
            root(0, sml[:, 8:10])
            act.wait_ge(lam_done, 1)
            act.activation(sml[:, 272:280], sml[:, 264:272], ACT.Exp, scale=-1.0).then_inc(rate_exp, 1)
            round_to(U_GATE + 3 + CV - 1)
            for n in range(2 * RC):
                m, c = n // RC, n % RC
                act.wait_ge(bd_ready, n + 1)
                act.activation((rg, ig)[m][:, c, :], bank[4 + n % 4][:, 0:S], ACT.Sigmoid,
                               bias=col[:, (C_BA, C_BX)[m] + c:(C_BA, C_BX)[m] + c + 1]).then_inc(gates_done, 1)
            round_to(U_GATE + 9 + CV - 1)
            act.wait_ge(l_done, 1)
            act.activation(ar[:, 8192:10240], ar[:, 4096:6144], ACT.Exp, scale=-1.0).then_inc(a_done, 1)
            round_to(U_GATE + 15 + CV - 1)
            act.wait_ge(st_free, 16)
            act.activation(ar[:, 12288:14336], ar[:, 12288:14336], ACT.Gelu_apprx_tanh).then_inc(gelu_done, 1)
            for m in range(6):
                round_to(U_QKV + 8 * m + 7 + CV - 1)
                act.wait_ge(unit_used, U_QKV + 8 * m + 8)
                for b in range(TB):
                    dst = qk[:, b, 512 * m:512 * m + 512] if m < 4 else vsb[:, b, 512 * (m - 4):512 * (m - 3)]
                    if m == 4 and b == 0:
                        act.wait_ge(rm_done, 1)
                    ins = act.activation(dst, bank[m % 2 * 2 + b][:], ACT.Copy, scale=sml[:, 8 + b:9 + b])
                ins.then_inc(mm_free, 1)
                if m == 0:
                    act.wait_ge(trig_ready, 1)
                    act.activation(sml[:, 128:192], sml[:, 64:128], ACT.Sin).then_inc(sin_done, 1)
                    root(1, naive)
                if m == 1:
                    act.wait_ge(rm_done, 1)
                    act.dma_start(madd, masks[0]).then_inc(mask_in, 16)
                    act.dma_start(mcnt, masks[1]).then_inc(mask_in, 16)
                    for c in range(RC):
                        act.activation(ig[:, c, :], gate[:, c, :], ACT.Copy,
                                       scale=col[:, C_GR + c:C_GR + c + 1]).then_inc(rm_gain, 1)
                    act.activation(rsq, ar[:, 12288:14336], ACT.Square).then_inc(rm_gain, 1)
                if m == 2:
                    root(2, sml[:, 26:28])

            for i in range(HEADS + 3):
                if i < HEADS:
                    round_to(U_OUTR + 2 * i + CV - 1)
                h = i - 1
                if 0 <= h < HEADS:
                    act.wait_ge(nmx_done, h + 1)
                    act.activation(sm[:, h % 2, 0:P], sm[:, h % 2, 0:P], ACT.Exp, scale=SCALE,
                                   bias=sml[:, 16 + 2 * (h % 2):17 + 2 * (h % 2)])
                    act.activation(sm[:, h % 2, P:384], sm[:, h % 2, P:384], ACT.Exp, scale=SCALE,
                                   bias=sml[:, 17 + 2 * (h % 2):18 + 2 * (h % 2)]).then_inc(exp_done, 1)
                h = i - 2
                if 0 <= h < HEADS:
                    act.wait_ge(pt_ready, h + 1)
                    if h >= 2:
                        act.wait_ge(pv_ready, h - 1)
                    act.activation(pt[:, h % 2, :], bank[6][:, 0:384], ACT.Copy).then_inc(pt_copied, 1)
                h = i - 3
                if 0 <= h < HEADS:
                    act.wait_ge(pv_ready, h + 1)
                    if h >= 2:
                        act.wait_ge(at_split, h - 1)
                    act.activation(at[:, h % 2, :], bank[7][:, 0:S], ACT.Copy,
                                   scale=col[:, C_GA + h:C_GA + h + 1])
                    act.activation(sqt[:, h % 2, :], bank[7][:, 0:S], ACT.Square).then_inc(pv_gain, 1)
                if i < HEADS:
                    round_to(U_OUTR + 2 * i + 1 + CV - 1)
            root(3, sml[:, 24:26])
            for c in range(4):
                round_to(U_OUTA + 4 * c + 3 + CV - 1)
                squares(1, M_OUTA + c, c)
                if c == 0:
                    act.dma_start(ar[:, 4096:6144], subkeys).then_inc(sk_in, 16)
                if c >= 1:
                    gains(1, C_FFN, range(4 * c - 4, 4 * c), turned)
            gains(1, C_FFN, range(12, 16), turned)
            root(4, sml[:, 10:12])
            round_to(U_WQ + CV - 1)
            for kk in range(KC // 2):
                act.wait_ge(xg_scaled, kk + 1)
                act.activation(xop[:, 2 * kk:2 * kk + 2, 0, :], xg[:, 2 * kk:2 * kk + 2, :], ACT.Copy).then_inc(xg_high, 1)
            for j in range(HC):
                round_to(U_WQ + 2 * j + 1 + CV - 1)
                act.wait_ge(unit_used, U_WQ + 2 * j + 2)
                if j >= 2:
                    act.wait_ge(key_ready, j - 1)
                act.activation(qt[:, j % 2, :], bank[j % 4][:, 0:S], ACT.Copy).then_inc(st_free, 1)

            def gelu_tile(g, j, n0):
                act.wait_ge(unit_used, n0 + 2 * j + 2)
                start = g % AHEAD * (GE * S) + j * S
                act.activation(ar[:, bass.ds(start, S)] if not isinstance(start, int) else ar[:, start:start + S],
                               bank[4 + j % 2][:, 0:S], ACT.Gelu_apprx_tanh).then_inc(ua_free, 1)

            def ahead(g):
                n0 = U_U0 + 2 * GE * g
                for j in range(GE):
                    for e in range(2):
                        off = 2 * j + e + CV - 1
                        round_unit(n0 + off, off % RAW, True)
                    gelu_tile(g, j, n0)

            act.wait_ge(key_ready, HC)
            with act.Fori(0, 2) as g:
                ahead(g)
            act.wait_ge(bm_done, TB)
            act.activation(ex, ex, ACT.Exp).then_inc(eg_done, 1)

            def spread(g, j, first):
                n0, c = U_U0 + 2 * GE * g, GE * (g - 2) + j
                for e in range(2):
                    off = 2 * j + e + CV - 1
                    round_unit(n0 + off, off % RAW, True)
                gelu_tile(g, j, n0)
                b = j % 2
                for s in range(4):
                    act.wait_ge(g_ready, 4 * c + s + 1)
                    if s == 0 and not (first and j < 2):
                        act.wait_ge(g_out[b], 8 * (c - b))
                    act.activation(stg[b].rearrange("p (i t) -> p t i", t=16)[:, 4 * s:4 * s + 4, :],
                                   bank[s][:].rearrange("p (t i) -> p t i", t=4), ACT.Copy).then_inc(g_copied, 1)
                act.wait_ge(g_copied, 4 * c + 4)
                act.dma_start(g_dram[:, :, c * P:c * P + P].rearrange("g p x -> p g x") if isinstance(c, int)
                              else g_dram[:, :, bass.ds(c * P, P)].rearrange("g p x -> p g x"),
                              stg[b].rearrange("p (g x) -> p g x", g=NG)).then_inc(g_out[b], 16)

            for j in range(GE):
                spread(2, j, True)
            for j in range(GE):
                spread(3, j, False)
            act.wait_ge(g_out[0], 128)
            act.wait_ge(g_out[1], 128)
            act.dma_start(gt, g_dram[0]).then_inc(g_in, 16)
            ahead(AHEAD - 1)

            def v_units(n0):
                for off in range(CV - 1, 16 + CV - 1):
                    round_unit(n0 + off, off % RAW, True)

            def next_weights(g):
                act.wait_ge(g_used, g)
                act.dma_start(gt, g_dram[bass.ds(g, 1)].rearrange("g p x -> p (g x)")).then_inc(g_in, 16)

            with act.Fori(0, NG - AHEAD) as g:
                next_weights(g + 1)
                n0 = U_VU + 32 * g
                v_units(n0)
                for j in range(GE):
                    for e in range(2):
                        off = 16 + 2 * j + e + CV - 1
                        round_unit(n0 + off, off % RAW, True)
                    gelu_tile(g + AHEAD, j, n0 + 16)
            with act.Fori(NG - AHEAD, NG - 1) as g:
                next_weights(g + 1)
                v_units(U_V1 + 16 * (g - (NG - AHEAD)))
            for off in range(CV - 1, 16 + CV - 1):
                round_unit(U_V1 + 16 * (AHEAD - 1) + off, off % RAW, False)
            made[0] = U_PROJ + CV - 1

            act.wait_ge(wexp_done, 4 * NG)
            act.dma_start(fnb, final_norm).then_inc(late_in, 16)
            act.dma_start(bias, b_gate).then_inc(late_in, 16)
            for c in range(4):
                squares(2, M_PROJ - 4 + c, c)
                round_to(U_PROJ + c + 1)
            for m in range(4):
                act.wait_ge(unit_used, U_PROJ + m + 1)
                for b in range(TB):
                    ins = act.activation(pp[:, b, 512 * m:512 * m + 512], bank[m % 2 * 2 + b][:], ACT.Copy)
                ins.then_inc(mm_free, 1)
                round_to(U_PROJ + 4 + m)
            gains(2, C_PLE, range(KC), turned)
            root(5, sml[:, 12:14])
            for m in range(4):
                round_to(U_PLE + 8 * m + 7 + CV - 1)
                act.wait_ge(mm_free, M_PLE + m + 1)
                act.activation(sg[:, m % 2], sg[:, m % 2], ACT.Sigmoid).then_inc(sig_done, 1)
                act.wait_ge(ple_done, m + 1)
                for b in range(TB):
                    ins = act.activation(xs[:, b, 512 * m:512 * m + 512], hres[:, b, 512 * m:512 * m + 512], ACT.Square,
                                         accum_out=sml[:, 32 + 4 * b + m:33 + 4 * b + m])
                ins.then_inc(ssq_done, 1)
            root(6, sml[:, 482:484])

        @block.tensor
        def _(pe):
            def wide(n, k, pair, x_of, first, last, loop=True):
                pe.wait_ge(lo_done, n + 1)
                for e in range(2):
                    xk = x_of(e)
                    for b in range(TB):
                        acc = bank[2 * pair + b][:]
                        wh, wl = hi[:, k, 512 * e:512 * e + 512], lo[:, k, 512 * e:512 * e + 512]
                        xh, xl = xk[:, 0, P * b:P * b + P], xk[:, 1, P * b:P * b + P]
                        pe.matmul(acc, xh, wh, start=first and e == 0, stop=False)
                        pe.matmul(acc, xh, wl, start=False, stop=False)
                        ins = pe.matmul(acc, xl, wh, start=False, stop=last and e == 1)
                ins.then_inc(unit_used, 1)

            def tall(n, k, acc, half, pairs=None):
                pe.wait_ge(lo_done, n + 1)
                for e in range(8):
                    if pairs is not None and e % 2 == 0:
                        pe.wait_ge(xt_split, pairs + 4 * half + e // 2 + 1)
                    xk = xop[:, 8 * half + e]
                    wh, wl = hi[:, k, P * e:P * e + P], lo[:, k, P * e:P * e + P]
                    pe.matmul(acc, wh, xk[:, 0, :], start=half == 0 and e == 0, stop=False)
                    pe.matmul(acc, wh, xk[:, 1, :], start=False, stop=False)
                    ins = pe.matmul(acc, wl, xk[:, 0, :], start=False, stop=half == 1 and e == 7)
                ins.then_inc(unit_used, 1)

            def chunk(m, n0, units, x_of, loop=False, pair=None, weights=None):
                pair = m % 2 if pair is None else pair
                if loop or m >= 2:
                    pe.wait_ge(mm_free, m - 1)
                for u in range(units):
                    if weights is not None:
                        pe.wait_ge(wexp_done, weights + u + 1)
                    wide(n0 + u, ((n0 if isinstance(n0, int) else 0) + u) % CV, pair, lambda e, u=u: x_of(2 * u + e),
                         u == 0, u == units - 1)

            def turn(n, c):
                for kk in (2 * c, 2 * c + 1):
                    if kk >= 4:
                        pe.wait_ge(xt_gain, 16 * n + 2 * kk - 6)
                    for e in range(2):
                        for b in range(TB):
                            k = 2 * kk + e
                            ins = pe.transpose(bank[4 + kk % 4][:, S * e + P * b:S * e + P * b + P],
                                               hres[:, b, P * k:P * k + P], idn[:])
                    ins.then_inc(xt_ready, 1)

            def broadcast(n):
                pe.wait_ge(diag_done, n + 1)
                if n:
                    pe.wait_ge(xt_gain, 2 * KC)
                for b in range(TB):
                    ins = pe.matmul(bank[7][:, P * b:P * b + P], ones[:], grest[:, P * b:P * b + P], start=True, stop=True)
                ins.then_inc(bc_ready, 1)

            pe.wait_ge(one_done, 1)
            for j in range(2 * RC):
                if j >= 4:
                    pe.wait_ge(st_free, j - 3)
                for u in range(2):
                    tall(U_XR + 2 * j + u, (2 * j + u) % CV, bank[j % 4][:, 0:S], u, 0 if j == 0 else None)
                if j == 1:
                    broadcast(0)
                if j == RC + 1:
                    pe.wait_ge(bd_in, 64)
                    pe.wait_ge(conv_done, 1)
                    for n in range(2 * RC):
                        if n >= 4:
                            pe.wait_ge(gates_done, n - 3)
                        pe.matmul(bank[4 + n % 4][:, 0:S], bd[:, n // RC, n % RC, :], xc[:, n % RC, :],
                                  start=True, stop=True).then_inc(bd_ready, 1)
            pe.wait_ge(st_free, 16)
            chunk(0, U_QKV, 8, lambda k: xop[:, k])
            chunk(1, U_QKV + 8, 8, lambda k: xop[:, k])
            chunk(2, U_QKV + 16, 8, lambda k: xop[:, k])
            pe.wait_ge(rm_gain, RC + 1)
            sq = rsq.rearrange("p (c t) -> p c t", c=RC)
            for b in range(TB):
                for c in range(RC):
                    ins = pe.matmul(bank[7][:, 256 + 2 * b:257 + 2 * b], sq[:, c, P * b:P * b + P], ones[:, 0:1],
                                    start=c == 0, stop=c == RC - 1)
            ins.then_inc(rsum_out, 1)
            for m in range(3, 6):
                chunk(m, U_QKV + 8 * m, 8, lambda k: xop[:, k])

            def side_unit(n):
                m, u = n // 4, n % 4
                if u == 0:
                    pe.wait_ge(mm_free, M_OUTR + m - 1)
                wide(U_OUTR + n, n % CV, m % 2, lambda e: rop[:, 2 * u + e], u == 0, u == 3)

            pe.wait_ge(const_in, 16 * N_CONST)
            pe.wait_ge(rnn_split, 1)
            for i in range(HEADS + 3):
                h = i
                if h < HEADS:
                    if h == 0:
                        pe.wait_ge(rope_done, 1)
                    else:
                        pe.wait_ge(ht_copied, h)
                    for q in range(2):
                        for b in range(TB):
                            ins = pe.transpose(bank[4][:, S * q + P * b:S * q + P * b + P],
                                               qk[:, b, A * q + P * h:A * q + P * h + P], idn[:])
                    ins.then_inc(ht_ready, 1)
                    side_unit(2 * i)
                h = i - 1
                if 0 <= h < HEADS:
                    pe.wait_ge(ht_copied, h + 1)
                    if h >= 1:
                        pe.wait_ge(sc_read, h)
                    qh, kh = qkt[:, h % 2, 0, :], qkt[:, h % 2, 1, :]
                    pe.matmul(bank[5][:, 0:P], qh[:, 0:P], kh[:, 0:P], start=True, stop=True)
                    pe.matmul(bank[5][:, P:384], qh[:, P:S], kh, start=True, stop=True).then_inc(sc_ready, 1)
                h = i - 2
                if 0 <= h < HEADS:
                    pe.wait_ge(prob_done, h + 1)
                    if h >= 1:
                        pe.wait_ge(pt_copied, h)
                    for j in range(3):
                        ins = pe.transpose(bank[6][:, P * j:P * j + P], sm[:, h % 2, P * j:P * j + P], idn[:])
                    ins.then_inc(pt_ready, 1)
                h = i - 3
                if 0 <= h < HEADS:
                    pe.wait_ge(pt_copied, h + 1)
                    pe.wait_ge(mm_free, 6)
                    if h >= 1:
                        pe.wait_ge(pv_gain, h)
                    v0, v1 = (vsb[:, b, P * h:P * h + P] for b in range(TB))
                    pr = pt[:, h % 2, :]
                    pe.matmul(bank[7][:, 0:P], v0, pr[:, 0:P], start=True, stop=True)
                    pe.matmul(bank[7][:, P:S], v0, pr[:, P:S], start=True, stop=False)
                    pe.matmul(bank[7][:, P:S], v1, pr[:, S:384], start=False, stop=True).then_inc(pv_ready, 1)
                if i < HEADS:
                    side_unit(2 * i + 1)
            pe.wait_ge(asum_ready, 1)
            for b in range(TB):
                ins = pe.matmul(bank[7][:, 256 + 2 * b:257 + 2 * b], sqsum[:, P * b:P * b + P], ones[:, 0:1],
                                start=True, stop=True)
            ins.then_inc(asum_out, 1)
            for c in range(4):
                chunk(M_OUTA + c, U_OUTA + 4 * c, 4, lambda k: xop[:, GE + k])
                if c >= 1:
                    pe.wait_ge(mm_free, M_OUTA + c)
                    turn(1, c - 1)
            pe.wait_ge(mm_free, M_V)
            turn(1, 3)
            broadcast(1)

            def key_scores(j):
                pe.wait_ge(st_free, 16 + j + 1)
                if j >= 2:
                    pe.wait_ge(key_read, j - 1)
                for b in range(TB):
                    ins = pe.matmul(bank[6 + j % 2][:, P * b:P * b + P], qt[:, j % 2, P * b:P * b + P],
                                    skey[:, j, :], start=True, stop=True)
                ins.then_inc(key_ready, 1)

            for j in range(HC):
                if j >= 4:
                    pe.wait_ge(st_free, 16 + j - 3)
                for u in range(2):
                    tall(U_WQ + 2 * j + u, (2 * j + u) % CV, bank[j % 4][:, 0:S], u, 8 if j == 0 else None)
                if j == 0:
                    pe.wait_ge(sk_in, 16)
                if j >= 2:
                    key_scores(j - 2)
            key_scores(HC - 2)
            key_scores(HC - 1)

            def expert_pair(n0, t, each=None):
                for b in range(2):
                    if not isinstance(t, int) or t + b >= 2:
                        pe.wait_ge(ua_free, t + b - 1)
                    for u in range(2):
                        tall(n0 + 2 * b + u, 2 * b + u, bank[4 + b][:, 0:S], u)
                    if each:
                        each(b)

            def spread(c, first):
                for s in range(4):
                    if s % 2 == 0:
                        pe.wait_ge(hot_done, 2 * c + s // 2 + 1)
                    if not first:
                        pe.wait_ge(g_copied, 4 * c + s - 3)
                    for k in range(4):
                        rows = hot[:, s // 2, :, :, 4 * (s % 2) + k]
                        for part in range(3):
                            ins = pe.matmul(bank[s][:, P * k:P * k + P], rows[:, 0], rows[:, 1 + part],
                                            start=part == 0, stop=part == 2)
                    ins.then_inc(g_ready, 1)

            expert_pair(U_U0, 0)
            with pe.Fori(1, GE) as i:
                expert_pair(U_U0 + 4 * i, 2 * i)
            for b in range(TB):
                pe.wait_ge(picked, b + 1)
                for q in range(3):
                    ins = pe.transpose(bank[6 + b][:, P * q:P * q + P], pick[:, b, q, :], idn[:])
                ins.then_inc(sel_ready, 1)
            expert_pair(U_U0 + 4 * GE, 2 * GE, lambda b: spread(b, b == 0))
            with pe.Fori(1, GE) as i:
                expert_pair(U_U0 + 4 * GE + 4 * i, 2 * GE + 2 * i, lambda b: spread(2 * i + b, False))
            with pe.Fori(0, GE // 2) as i:
                expert_pair(U_U0 + 8 * GE + 4 * i, 4 * GE + 2 * i)
            pe.wait_ge(g_copied, 64)

            def values(g, n0):
                with pe.Fori(0, 2) as q:
                    for e in range(2):
                        chunk(M_V + 4 * g + 2 * q + e, n0 + 8 * q + 4 * e, 4, lambda k: wop[:, k], True, e,
                              weights=4 * g)

            with pe.Fori(0, NG - AHEAD) as g:
                values(g, U_VU + 32 * g)
                with pe.Fori(0, GE // 2) as q:
                    expert_pair(U_VU + 32 * g + 16 + 4 * q, GE * (g + AHEAD) + 2 * q)
            with pe.Fori(NG - AHEAD, NG) as g:
                values(g, U_V1 + 16 * (g - (NG - AHEAD)))

            for m in range(4):
                chunk(M_PROJ + m, U_PROJ + m, 1, lambda k: pop[:, k])
            for c in range(4):
                turn(2, c)
            pe.wait_ge(xt_split, 24)
            for m in range(4):
                chunk(M_PLE + m, U_PLE + 8 * m, 8, lambda k: xop[:, k])

        @block.vector
        def _(dve):
            steps, issued = [0], [0]

            def link(ins):
                steps[0] = steps[0] + 1
                issued[0] += 1
                ins.then_inc(dve_step, 1)
                dve.wait_ge(dve_step, steps[0])

            def ts(out_, in_, s1, s2, op0, op1=ALU.bypass):
                return dve.tensor_scalar(out_, in_, s1, s2, op0, op1)

            def tt(out_, a_, b_, op):
                return dve.tensor_tensor(out_, a_, b_, op)

            def stt(out_, a_, s_, b_, op0, op1, **kw):
                return dve.scalar_tensor_tensor(out_, a_, s_, b_, op0, op1, **kw)

            def rstd(n, dst, src, width):
                ts(dst, src, 1.0 / width, EPS, ALU.mult, ALU.add).then_inc(mean_done, 1)
                dve.wait_ge(root_done, n + 1)
                link(dve.reciprocal(dst, dst))

            def split_pair(n, kk):
                dve.wait_ge(xt_gain, 16 * n + 2 * kk + 2)
                src = tmp[:, kk % 2]
                link(dve.tensor_copy(xop[:, 2 * kk:2 * kk + 2, 0, :], src))
                tt(xop[:, 2 * kk:2 * kk + 2, 1, :], src, xop[:, 2 * kk:2 * kk + 2, 0, :].bitcast(F32),
                   ALU.subtract).then_inc(xt_split, 1)

            def diagonal(n, r):
                for b in range(TB):
                    ins = ts(grest[:, P * b:P * b + P], idn[:], r[:, b:b + 1], None, ALU.mult)
                ins.then_inc(diag_done, 1)
                dve.wait_ge(bc_ready, n + 1)
                link(dve.tensor_copy(bc[:], bank[7][:, 0:S]))

            def scale_tile(dst, src, sem_):
                tt(dst, src, bc[:], ALU.mult).then_inc(sem_, 1)

            dve.memset(rtmp[:, 1, :], 0.0).then_inc(bd_zero, 1)
            for kk in range(KC // 2):
                split_pair(0, kk)
            dve.wait_ge(const_in, 16 * N_CONST)
            link(ts(sml[:, 280:288], col[:, C_LAM:C_LAM + RC], -1.0, None, ALU.mult))
            link(tt(sml[:, 264:272], col[:, C_LAM:C_LAM + RC], sml[:, 280:288], ALU.max))
            ts(sml[:, 280:288], sml[:, 280:288], 0.0, None, ALU.max).then_inc(lam_done, 1)
            link(dve.tensor_copy(pop[:, :, 0, :], praw))
            tt(pop[:, :, 1, :], praw, pop[:, :, 0, :].bitcast(F32), ALU.subtract).then_inc(pop_done, 1)
            dve.wait_ge(pop_done, 1)
            dve.wait_ge(ssq_done, 2)
            rstd(0, sml[:, 8:10], sml[:, 0:2], D)
            diagonal(0, sml[:, 8:10])
            for c in range(RC):
                dve.wait_ge(unit_used, U_XR + 2 * c + 2)
                scale_tile(xr[:, c, :], bank[c % 4][:, 0:S], st_free)
                dve.wait_ge(st_free, c + 1)
                link(ts(xc[:, c, :], xr[:, c, :], col[:, C_CW + 3 * RC + c:C_CW + 3 * RC + c + 1],
                        col[:, C_CB + c:C_CB + c + 1], ALU.mult, ALU.add))
                for k in range(TAPS - 1):
                    lag = TAPS - 1 - k
                    ins = stt(xc[:, c, lag:S], xr[:, c, 0:S - lag], col[:, C_CW + k * RC + c:C_CW + k * RC + c + 1],
                              xc[:, c, lag:S], ALU.mult, ALU.add)
                    if k < TAPS - 2:
                        link(ins)
                    elif c == RC - 1:
                        ins.then_inc(conv_done, 1)

            def gate_tile(c):
                dve.wait_ge(unit_used, U_GATE + 2 * c + 2)
                scale_tile(gate[:, c, :], bank[c % 4][:, 0:S], st_free)

            dve.wait_ge(rate_exp, 1)
            e_, z_, z2, pz = (sml[:, o:o + 8] for o in (272, 288, 296, 304))
            link(ts(z_, e_, 2.0, None, ALU.add))
            link(dve.reciprocal(z2, z_))
            link(tt(z_, e_, z2, ALU.mult))
            link(tt(z2, z_, z_, ALU.mult))
            link(ts(pz, z2, 1.0 / 17, 1.0 / 15, ALU.mult, ALU.add))
            for k in (13, 11, 9, 7, 5, 3, 1):
                link(tt(pz, pz, z2, ALU.mult))
                link(ts(pz, pz, 1.0 / k, None, ALU.add))
            link(tt(pz, pz, z_, ALU.mult))
            link(stt(pz, pz, 2.0, sml[:, 280:288], ALU.mult, ALU.add))
            rate = sml[:, 256:264]
            link(ts(rate, pz, RGLRU_C, None, ALU.mult))
            gate_tile(0)
            gate_tile(1)
            dve.wait_ge(gates_done, 2 * RC)
            lw, aw, iw, xw = ar[:, 4096:6144], ar[:, 8192:10240], ar[:, 6144:8192], rtmp[:, 0, :]
            tt(rg, rg, rate.unsqueeze(2).to_broadcast([P, RC, S]), ALU.mult).then_inc(l_done, 1)
            link(tt(iw, iw, xw, ALU.mult))
            dve.wait_ge(l_done, 1)
            yw = xw
            link(ts(yw, lw, 2.0, 0.25, ALU.mult, ALU.min))
            gate_tile(2)
            link(ts(poly, yw, -1.0 / 720, None, ALU.mult))
            for k, f in enumerate((1.0 / 120, -1.0 / 24, 1.0 / 6, -0.5, 1.0)):
                link(stt(poly, poly, f, yw, ALU.add, ALU.mult))
                if k % 2 == 1:
                    gate_tile(3 + k // 2)
            dve.wait_ge(a_done, 1)
            link(tt(naive, aw, aw, ALU.mult))
            link(ts(naive, naive, -1.0, 1.0, ALU.mult, ALU.add))
            gate_tile(5)
            link(ts(yw, yw, 0.25, None, ALU.is_lt))
            dve.copy_predicated(naive, yw.bitcast(U32), poly).then_inc(mean_done, 1)
            gate_tile(6)
            gate_tile(7)
            ang, arg, trn = sml[:, 64:128], sml[:, 192:256], sml[:, 320:384]
            link(dve.tensor_copy(sml[:, 20:22], posi[:]))
            for b in range(TB):
                link(ts(arg[:, ROT * b:ROT * b + ROT], col[:, C_FREQ:C_FREQ + ROT], sml[:, 20 + b:21 + b], None, ALU.mult))
            link(dve.tensor_copy(arg[:, 32:64], arg[:, 0:32]))
            link(ts(trn[:, 0:32], arg[:, 0:32], 1.0 / TAU, None, ALU.mult))
            link(ts(trn[:, 32:64], arg[:, 32:64], 1.0 / TAU, 0.25, ALU.mult, ALU.add))
            link(ts(trn, trn, ROUND, None, ALU.add))
            link(ts(trn, trn, ROUND, None, ALU.subtract))
            link(stt(ang, trn, -TAU1, arg, ALU.mult, ALU.add))
            link(stt(ang, trn, -TAU2, ang, ALU.mult, ALU.add))
            link(stt(ang, trn, -TAU3, ang, ALU.mult, ALU.add))
            link(ts(ang[:, 32:64], ang[:, 32:64], TAU / 4, None, ALU.add))
            ts(ang, ang, 3.1415925, -3.1415925, ALU.min, ALU.max).then_inc(trig_ready, 1)
            dve.wait_ge(root_done, 2)
            link(tt(iw, iw, naive, ALU.mult))
            for c in range(RC):
                ins = dve.tensor_tensor_scan(rg[:, c, :], av[:, c, :], ig[:, c, :], 0.0, ALU.mult, ALU.add)
            link(ins)
            dve.wait_ge(gelu_done, 1)
            tt(ar[:, 12288:14336], lw, ar[:, 12288:14336], ALU.mult).then_inc(rm_done, 1)
            dve.wait_ge(rm_gain, RC)
            for k in range(2):
                link(dve.tensor_copy(rop[:, 4 * k:4 * k + 4, 0, :], ig[:, 4 * k:4 * k + 4, :]))
                ins = tt(rop[:, 4 * k:4 * k + 4, 1, :], ig[:, 4 * k:4 * k + 4, :],
                         rop[:, 4 * k:4 * k + 4, 0, :].bitcast(F32), ALU.subtract)
            ins.then_inc(rnn_split, 1)
            dve.wait_ge(rsum_out, 1)
            rstd_a, rstd_r = sml[:, 24:26], sml[:, 26:28]
            sums = bank[7][:, 256:260].rearrange("p (b e) -> p b e", e=2)[:, :, 0]
            rstd(2, rstd_r, sums, A)

            def add_mixed(m, end, r):
                dve.wait_ge(unit_used, end)
                o = 512 * ((m - M_OUTR) % 4)
                for b in range(TB):
                    ins = stt(hres[:, b, o:o + 512], bank[m % 2 * 2 + b][:], r[:, b:b + 1], hres[:, b, o:o + 512],
                              ALU.mult, ALU.add)
                ins.then_inc(mm_free, 1)

            dve.wait_ge(mm_free, 4)
            dve.wait_ge(sin_done, 1)
            for b in range(TB):
                rows = qk[:, b, :].rearrange("p (h d) -> p h d", d=P)
                x1, x2 = rows[:, :, 0:ROT], rows[:, :, ROT:2 * ROT]
                sn = sml[:, 128 + ROT * b:144 + ROT * b].unsqueeze(1).to_broadcast([P, 16, ROT])
                cs = sml[:, 160 + ROT * b:176 + ROT * b].unsqueeze(1).to_broadcast([P, 16, ROT])
                t1, t2 = (tmp[:, b, e].rearrange("p (h d) -> p h d", d=ROT) for e in range(2))
                tt(t1, x1, sn, ALU.mult)
                link(tt(t2, x2, sn, ALU.mult))
                tt(x1, x1, cs, ALU.mult)
                link(tt(x2, x2, cs, ALU.mult))
                tt(x1, x1, t2, ALU.subtract)
                link(tt(x2, x2, t1, ALU.add))
            dve.sem_inc(rope_done, 1)

            dve.wait_ge(mask_in, 32)
            for i in range(HEADS + 3):
                if i in (2, 4, 6, 8):
                    add_mixed(M_OUTR + i // 2 - 1, U_OUTR + 2 * i, rstd_r)
                h = i
                if h < HEADS:
                    dve.wait_ge(ht_ready, h + 1)
                    if h >= 2:
                        dve.wait_ge(sc_ready, h - 1)
                    dve.tensor_copy(ar[:, 6144 + 512 * (h % 2):6656 + 512 * (h % 2)], bank[4][:]).then_inc(ht_copied, 1)
                h = i - 1
                if 0 <= h < HEADS:
                    dve.wait_ge(sc_ready, h + 1)
                    if h >= 2:
                        dve.wait_ge(pt_ready, h - 1)
                    s_, st = sm[:, h % 2, :], 2 * (h % 2)
                    ins = tt(s_, bank[5][:, 0:384], madd, ALU.add)
                    ins.then_inc(sc_read, 1)
                    dve.wait_ge(sc_read, h + 1)
                    dve.tensor_reduce(sml[:, 400 + st:401 + st], s_[:, 0:P], AX_X, ALU.max)
                    link(dve.tensor_reduce(sml[:, 401 + st:402 + st], s_[:, P:384], AX_X, ALU.max))
                    ts(sml[:, 16 + st:18 + st], sml[:, 400 + st:402 + st], -SCALE, None, ALU.mult).then_inc(nmx_done, 1)
                    dve.wait_ge(exp_done, h + 1)
                    stt(s_[:, 0:P], s_[:, 0:P], 1.0, mcnt[:, 0:P], ALU.mult, ALU.mult, accum_out=sml[:, 404 + st:405 + st])
                    link(stt(s_[:, P:384], s_[:, P:384], 1.0, mcnt[:, P:384], ALU.mult, ALU.mult,
                             accum_out=sml[:, 405 + st:406 + st]))
                    link(dve.reciprocal(sml[:, 408 + st:410 + st], sml[:, 404 + st:406 + st]))
                    ts(s_[:, 0:P], s_[:, 0:P], sml[:, 408 + st:409 + st], None, ALU.mult)
                    ts(s_[:, P:384], s_[:, P:384], sml[:, 409 + st:410 + st], None, ALU.mult).then_inc(prob_done, 1)
                h = i - 3
                if 0 <= h < HEADS:
                    dve.wait_ge(pv_gain, h + 1)
                    if h == 0:
                        link(dve.tensor_copy(sqsum, sqt[:, 0, :]))
                    else:
                        link(tt(sqsum, sqsum, sqt[:, h % 2, :], ALU.add))
                    link(dve.tensor_copy(xop[:, GE + h, 0, :], at[:, h % 2, :]))
                    tt(xop[:, GE + h, 1, :], at[:, h % 2, :], xop[:, GE + h, 0, :].bitcast(F32),
                       ALU.subtract).then_inc(at_split, 1)
            dve.sem_inc(asum_ready, 1)
            dve.wait_ge(asum_out, 1)
            rstd(3, rstd_a, sums, A)
            for c in range(4):
                add_mixed(M_OUTA + c, U_OUTA + 4 * c + 4, rstd_a)

            def mean_square(r):
                link(dve.tensor_reduce(r, sml[:, 32:40].rearrange("p (b m) -> p b m", b=TB), AX_X, ALU.add))

            dve.wait_ge(ssq_done, 2 + 4)
            mean_square(sml[:, 10:12])
            rstd(4, sml[:, 10:12], sml[:, 10:12], D)
            diagonal(1, sml[:, 10:12])

            for kk in range(KC // 2 + 1):
                if kk < KC // 2:
                    two = xg[:, 2 * kk:2 * kk + 2, :]
                    if kk == 0:
                        dve.wait_ge(xt_gain, 2 * KC)
                    tt(two, two, bc[:].unsqueeze(1).to_broadcast([P, 2, S]), ALU.mult).then_inc(xg_scaled, 1)
                if kk >= 1:
                    dve.wait_ge(xg_high, kk)
                    tt(xop[:, 2 * kk - 2:2 * kk, 1, :], xg[:, 2 * kk - 2:2 * kk, :],
                       xop[:, 2 * kk - 2:2 * kk, 0, :].bitcast(F32), ALU.subtract).then_inc(xt_split, 1)

            def top16(vals, work, last):
                for v, w_, t, ix in vals:
                    ins = dve.max(t[:, 0:8], v)
                link(ins)
                for v, w_, t, ix in vals:
                    dve.max_index(ix[:, 0:8], t[:, 0:8], v)
                for v, w_, t, ix in vals:
                    ins = dve.match_replace(w_, t[:, 0:8], v, NEG)
                if last is not None:
                    ins.then_inc(last, 1)
                    dve.wait_ge(last, last_at[0])
                else:
                    link(ins)
                for v, w_, t, ix in vals:
                    ins = dve.max(t[:, 8:16], w_)
                link(ins)
                for v, w_, t, ix in vals:
                    ins = dve.max_index(ix[:, 8:16], t[:, 8:16], w_)
                return ins

            last_at = [0]
            for j in range(HC):
                dve.wait_ge(key_ready, j + 1)
                last_at[0] = j + 1
                ins = top16([(bank[6 + j % 2][:, P * b:P * b + P], tkw[:, b, 0:P], tks[:, b, j, :], tki[:, b, j, :])
                             for b in range(TB)], None, key_read)
            link(ins)
            link(dve.tensor_copy(ar[:, 9216:9728], ar[:, 8704:9216].bitcast(U32)))

            for b in range(TB):
                s2 = tks[:, b].rearrange("p (h c) k -> p h c k", c=2)
                i2 = tkf[:, b].rearrange("p (h c) k -> p h c k", c=2)
                link(tt(cand, s2[:, :, 0, :].unsqueeze(3).to_broadcast([P, PH, TOPK, TOPK]),
                        s2[:, :, 1, :].unsqueeze(2).to_broadcast([P, PH, TOPK, TOPK]), ALU.add))
                pb = pos[:, b, :].rearrange("p (h k) -> p h k", k=TOPK)
                for hp in range(PH // 2):
                    ins = top16([(cand[:, h].rearrange("p a b -> p (a b)"), tkw[:, h % 2, :], best[:, b, h, :], pb[:, h, :])
                                 for h in (2 * hp, 2 * hp + 1)], None, None)
                    if hp < PH // 2 - 1:
                        link(ins)
                exb = ex[:, b, :].rearrange("p (h k) -> p h k", k=TOPK)
                link(ins)
                tt(exb, best[:, b], best[:, b, :, 0:1].to_broadcast([P, PH, TOPK]), ALU.subtract).then_inc(bm_done, 1)
                qd = tmp[:, 1, :, 0:P]
                link(ts(eq[:, 0:1].rearrange("p n a b -> p (n a b)")[:, 0:P].bitcast(U32), pos[:, b, :], 4, None,
                        ALU.logical_shift_right))
                link(dve.tensor_copy(qd[:, 0, :], eq[:, 0:1].rearrange("p n a b -> p (n a b)")[:, 0:P].bitcast(U32)))
                link(ts(eq[:, 0:1].rearrange("p n a b -> p (n a b)")[:, 0:P].bitcast(U32), pos[:, b, :], 15, None,
                        ALU.bitwise_and))
                link(dve.tensor_copy(qd[:, 1, :], eq[:, 0:1].rearrange("p n a b -> p (n a b)")[:, 0:P].bitcast(U32)))
                for q in range(2):
                    flat = eq.rearrange("p n a b -> p (n a) b")
                    link(tt(flat, qd[:, q, :].unsqueeze(2).to_broadcast([P, P, TOPK]),
                            iot[:, 0:TOPK].unsqueeze(1).to_broadcast([P, P, TOPK]), ALU.is_equal))
                    link(tt(eq, eq, i2[:, :, q, :].unsqueeze(2).to_broadcast([P, PH, TOPK, TOPK]), ALU.mult))
                    link(dve.tensor_reduce(pick[:, b, q, :], flat, AX_X, ALU.add))
            dve.wait_ge(eg_done, 1)
            for b in range(TB):
                exb = ex[:, b, :].rearrange("p (h k) -> p h k", k=TOPK)
                link(dve.tensor_reduce(sml[:, 416:424], exb, AX_X, ALU.add))
                link(dve.reciprocal(sml[:, 424:432], sml[:, 416:424]))
                tt(pick[:, b, 2, :].rearrange("p (h k) -> p h k", k=TOPK), exb,
                   sml[:, 424:432].unsqueeze(2).to_broadcast([P, PH, TOPK]), ALU.mult).then_inc(picked, 1)
            dve.tensor_copy(irep, iot[:].unsqueeze(2).to_broadcast([P, P, 8]))
            for b in range(TB):
                dve.wait_ge(sel_ready, b + 1)
                dve.tensor_copy(keyb[:, :, P * b:P * b + P], bank[6 + b][:, 0:S].rearrange("p (q t) -> p q t", q=2))
                link(dve.tensor_copy(grest[:, P * b:P * b + P], bank[6 + b][:, S:384]))
            for part in range(3):
                link(dve.tensor_copy(gpart[:, part, :], grest[:]))
                if part < 2:
                    link(tt(grest[:], grest[:], gpart[:, part, :], ALU.subtract))

            def hot_rows(q, b):
                at_ = bass.ds(8 * q, 8) if not isinstance(q, int) else slice(8 * q, 8 * q + 8)
                if not isinstance(q, int) or q >= 2:
                    dve.wait_ge(g_ready, 2 * q - 2)

                def over(row):
                    return row.unsqueeze(1).to_broadcast([P, P, 8])

                tt(hot[:, b, 0], irep, over(keyb[:, 1, at_]), ALU.is_equal)
                link(tt(eqb[:, b], irep, over(keyb[:, 0, at_]), ALU.is_equal))
                for part in range(3):
                    ins = tt(hot[:, b, 1 + part], eqb[:, b], over(gpart[:, part, at_]), ALU.mult)
                ins.then_inc(hot_done, 1)

            for b in range(2):
                hot_rows(b, b)
            start = steps[0]
            with dve.Fori(1, S // 16) as i:
                steps[0] = start + 2 * (i - 1)
                for b in range(2):
                    hot_rows(2 * i + b, b)
            steps[0] = start + 2 * (S // 16 - 1)

            def weigh(g):
                dve.wait_ge(g_in, 16 * g + 16)
                a4 = ar[:, bass.ds(g % AHEAD * (GE * S), GE * S)].rearrange("p (j c t) -> p j c t", j=GE, t=16)
                tt(a4, a4, gt.rearrange("p (c j t) -> p j c t", j=GE, t=16), ALU.mult).then_inc(g_used, 1)

            def split_weights(g, n0):
                dve.wait_ge(g_used, g + 1)
                w3 = ar[:, bass.ds(g % AHEAD * (GE * S), GE * S)].rearrange("p (j t) -> p j t", t=S)
                for u in range(4):
                    if n0 is not None:
                        dve.wait_ge(unit_used, n0 + u + 1)
                    two = slice(2 * u, 2 * u + 2)
                    link(ts(wop[:, two, 0, :], w3[:, two, :], 1.0, None, ALU.mult))
                    tt(wop[:, two, 1, :], w3[:, two, :], wop[:, two, 0, :].bitcast(F32),
                       ALU.subtract).then_inc(wexp_done, 1)

            def add_values(n0, chunks):
                for c in chunks:
                    dve.wait_ge(unit_used, n0 + 4 * c + 4)
                    for b in range(TB):
                        ins = tt(hres[:, b, 512 * c:512 * c + 512], bank[c % 2 * 2 + b][:],
                                 hres[:, b, 512 * c:512 * c + 512], ALU.add)
                    ins.then_inc(mm_free, 1)

            dve.wait_ge(g_ready, 64)
            dve.wait_ge(ua_free, GE)
            weigh(0)
            split_weights(0, None)

            def between(g, n0, wait):
                add_values(n0, (0, 1))
                if wait:
                    dve.wait_ge(ua_free, GE * (g + 2))
                weigh(g + 1)
                add_values(n0, (2,))
                split_weights(g + 1, n0 + 12)
                add_values(n0, (3,))

            start = steps[0]
            with dve.Fori(0, NG - AHEAD) as g:
                steps[0] = start + 4 * g
                between(g, U_VU + 32 * g, True)
            start = start + 4 * (NG - AHEAD)
            with dve.Fori(NG - AHEAD, NG - 1) as g:
                steps[0] = start + 4 * (g - (NG - AHEAD))
                between(g, U_V1 + 16 * (g - (NG - AHEAD)), False)
            steps[0] = start + 4 * (AHEAD - 1)
            add_values(U_V1 + 16 * (AHEAD - 1), range(4))

            for kk in range(KC // 2):
                split_pair(2, kk)
            dve.wait_ge(ssq_done, 2 + 4 + 4)
            mean_square(sml[:, 12:14])
            rstd(5, sml[:, 12:14], sml[:, 12:14], D)
            dve.wait_ge(late_in, 32)
            for m in range(4):
                dve.wait_ge(unit_used, U_PLE + 8 * m + 8)
                for b in range(TB):
                    ins = stt(sg[:, m % 2, b, :], bank[m % 2 * 2 + b][:], sml[:, 12 + b:13 + b],
                              bias[:, 512 * m:512 * m + 512], ALU.mult, ALU.add)
                ins.then_inc(mm_free, 1)
                dve.wait_ge(sig_done, m + 1)
                link(tt(sg[:, m % 2], sg[:, m % 2], pp[:, :, 512 * m:512 * m + 512], ALU.mult))
                tt(hres[:, :, 512 * m:512 * m + 512], hres[:, :, 512 * m:512 * m + 512], sg[:, m % 2],
                   ALU.add).then_inc(ple_done, 1)
            dve.wait_ge(ssq_done, 2 + 4 + 4 + 4)
            mean_square(sml[:, 482:484])
            rstd(6, sml[:, 482:484], sml[:, 482:484], D)
            for b in range(TB):
                for e in range(2):
                    half = slice(1024 * e, 1024 * e + 1024)
                    stt(xs[:, b, half], hres[:, b, half], sml[:, 482 + b:483 + b], fnb[:, half],
                        ALU.mult, ALU.mult).then_inc(y_done, 1)


_OUT = (1, S, D)


def wide_units(w, n0, n1):
    k, n = w.shape
    t = w.reshape(k // 256, 2, P, n // 512, 512).transpose(3, 0, 2, 1, 4)
    return t.reshape(-1, P, UW)[n0:n1]


def tall_units(w):
    k, n = w.shape
    return w.reshape(k // 1024, 8, P, n // P, P).transpose(3, 0, 2, 1, 4).reshape(-1, P, UW)


def kernel(**inputs):
    import concourse.bacc as bacc
    from concourse.bass_utils import run_bass_kernel_spmd

    a = {n: np.asarray(v) for n, v in inputs.items()}
    w_in, w_out = a["w_in"][0], a["w_out"][0]
    u, v = a["peer_u"][0], a["peer_v"][0]
    u_groups = tall_units(u.T).reshape(NG, 16, P, UW)
    v_groups = (v.reshape(NG, 4, 2, P, 4, 512).transpose(0, 4, 1, 3, 2, 5).reshape(NG, 16, P, UW))
    parts = [tall_units(w_in[:, 3 * A:]), wide_units(w_in[:, 0:3 * A], 0, 48),
             wide_units(w_out[A:], 0, 16), wide_units(w_out[0:A], 0, 16), tall_units(a["peer_wq"][0])]
    parts += [u_groups[g] for g in range(AHEAD)]
    for g in range(NG - AHEAD):
        parts += [v_groups[g], u_groups[g + AHEAD]]
    parts += [v_groups[g] for g in range(NG - AHEAD, NG)]
    parts += [wide_units(a["ple_proj"][0], 0, 4), wide_units(a["ple_w_gate"][0], 0, 32)]
    stream = np.concatenate(parts)

    def by_channel(t):
        return t.reshape(-1, P).T

    half = np.arange(ROT, dtype=np.float32)
    freq = (np.float32(500000.0) ** (-half * np.float32(2.0) / np.float32(2 * ROT))).astype(np.float32)
    cols = np.concatenate([by_channel(a["mix_norm"][0]), by_channel(a["ffn_norm"][0]), by_channel(a["ple_norm"][0]),
                           by_channel(a["attn_out_norm"][0]), by_channel(a["rnn_out_norm"][0]),
                           by_channel(a["conv_w"][0]), by_channel(a["conv_b"][0]), by_channel(a["rg_ba"][0]),
                           by_channel(a["rg_bx"][0]), by_channel(a["rg_lambda"][0]),
                           np.broadcast_to(freq, (P, ROT))], axis=1)
    lag = np.arange(S)[:, None] - np.arange(S)[None, :]
    count = (lag >= 0) * ((lag <= 128) * 1.0 + (lag % 4 == 0) + (lag % 16 == 0))
    count = np.concatenate([count[0:P, 0:P], count[P:]], axis=1).astype(np.float32)
    masks = np.stack([np.where(count > 0, 0.0, MASKED).astype(np.float32), count])
    arrays = {
        "stream": stream, "x": a["x"][0], "x_t": a["x"][0].T.reshape(KC, P, S).transpose(1, 0, 2),
        "positions": a["positions"][0].reshape(TB, P).T, "cols": cols, "masks": masks,
        "w_a": a["rg_wa"][0], "w_x": a["rg_wx"][0],
        "subkeys": a["peer_subkeys"][0].reshape(HC, KEYS, P).transpose(2, 0, 1).reshape(P, HC * KEYS),
        "p_t": a["p"][0, 0].T.reshape(2, P, S).transpose(1, 0, 2), "b_gate": np.broadcast_to(a["ple_b_gate"], (P, D)),
        "final_norm": np.broadcast_to(a["final_norm"], (P, D)),
        "iota": np.broadcast_to(np.arange(P, dtype=np.float32), (P, P)), "ident": np.eye(P, dtype=np.float32),
    }
    arrays = {n: np.ascontiguousarray(t) for n, t in arrays.items()}
    nc = bacc.Bacc("TRN2", target_bir_lowering=False, num_devices=1)
    aps = {n: nc.dram_tensor(f"in_{n}", t.shape, mybir.dt.from_np(t.dtype), kind="ExternalInput").ap()
           for n, t in arrays.items()}
    g_dram = nc.dram_tensor("spread", (NG, P, 16 * P), F32, kind="Internal").ap()
    out = nc.dram_tensor("out", (S, D), F32, kind="ExternalOutput").ap()
    build(nc, **aps, g_dram=g_dram, out=out)
    r = run_bass_kernel_spmd(nc, [{f"in_{n}": t for n, t in arrays.items()}], core_ids=[0])
    return r.results[0]["out"].reshape(_OUT)
```

```python
from contextlib import ExitStack

import numpy as np
import concourse.bass as bass
from concourse import mybir

ALU = mybir.AluOpType
ACT = mybir.ActivationFunctionType
AX_X = mybir.AxisListType.X
F32 = mybir.dt.float32
BF16 = mybir.dt.bfloat16
F32R = mybir.dt.float32r
I32 = mybir.dt.int32
U32 = mybir.dt.uint32

P = 128
S = 256
TB = S // P
D = 2048
KC = D // P
HEADS = 8
A = HEADS * P
RC = 8
ROT = 16
SCALE = float(P) ** -0.5
EPS = 1e-6
TAPS = 4
RGLRU_C = 8.0
PH = 8
HC = 2 * PH
KEYS = 128
TOPK = 16
SLOTS = PH * TOPK
NEG = -3.0e38
MASKED = -1.0e30

UW = 1024
RAW = 8
CV = 4
GE = 8
NG = 128 // GE
AHEAD = 5
U_XR = 0
U_GATE = U_XR + 16
U_QKV = U_GATE + 16
U_OUTR = U_QKV + 48
U_OUTA = U_OUTR + 16
U_PROJ = U_OUTA + 16
U_WQ = U_PROJ + 4
U_U0 = U_WQ + 32
U_VU = U_U0 + 16 * AHEAD
U_V1 = U_VU + 32 * (NG - AHEAD)
U_LAST = U_V1 + 16 * (AHEAD - 1)
U_PLE = U_LAST + 16
UNITS = U_PLE + 32
M_OUTR, M_OUTA, M_PROJ, M_V = 6, 10, 14, 18
M_PLE = M_V + 4 * NG
C_MIX, C_FFN, C_PLE = 0, 16, 32
C_GA, C_GR, C_CW, C_CB, C_BA, C_BX, C_LAM = 48, 56, 64, 96, 104, 112, 120
C_FREQ = 128
C_END = 144
BESIDE2 = (0, 1, 8, 9, 10)
TAU = 6.283185307179586
TAU1 = 6.28125
TAU2 = 0.0019350051879882812
TAU3 = 3.019915981956753e-07
ROUND = 12582912.0


def beside1(i):
    return i + sum(1 for e in BESIDE2 if e < i)


def build(nc, stream, x, x_t, positions, cols, masks, w_a, w_x, subkeys, p_t, b_gate, final_norm, iota, ident, g_dram, held, out):
    ctx = ExitStack()
    with ctx:
        def sb(name, shape, dt=F32):
            return ctx.enter_context(nc.sbuf_tensor(name, shape, dt))

        def sem(name):
            return ctx.enter_context(nc.semaphore(name))

        bank = [ctx.enter_context(nc.psum_tensor(f"bank{i}", [P, 512], F32)) for i in range(8)]
        xop = sb("xop", [P, KC, 2, S], F32R)
        with nc.sbuf_tensor("rtmp", [P, 2, D], F32) as rtmp:
            pass
        with nc.sbuf_tensor("rop", [P, GE, 2, S], F32R) as rop:
            pass
        with nc.sbuf_tensor("hot", [P, 2, 4, P, 8], BF16) as hot:
            pass
        wop = sb("wop", [P, GE, 2, S], F32R)
        pop = sb("pop", [P, 2, 2, S], F32R)
        hi = sb("hi", [P, CV, UW], F32R)
        lo = sb("lo", [P, CV, UW], F32R)
        raw = sb("raw", [P, RAW, UW])
        hres = sb("hres", [P, TB, D])
        arena = sb("arena", [P, 14336])
        idn = sb("idn", [P, P])
        iot = sb("iot", [P, P])
        col = sb("col", [P, C_END])
        ones = sb("ones", [P, P])
        sml = sb("sml", [P, 512])
        posi = sb("posi", [P, TB], I32)
        tmp = sb("tmp", [P, 2, 2, S])
        pick = sb("pick", [P, 2, 3, P])
        pos = sb("pos", [P, 2, P], U32)
        keyb = sb("keyb", [P, 2, S], BF16)
        gpart = sb("gpart", [P, 3, S], BF16)
        bc = sb("bc", [P, S])
        grest = sb("grest", [P, S])

        sqt, sqsum = tmp[:, 0], tmp[:, 1, 0]
        qt, tkw = tmp[:, 0], tmp[:, 1]

        ar = arena
        xs = ar[:, 0:4096].rearrange("p (b d) -> p b d", b=TB)
        xtr = ar[:, 0:4096].rearrange("p (k t) -> p k t", k=KC)
        qk = xs
        vsb = ar[:, 4096:6144].rearrange("p (b d) -> p b d", b=TB)
        qkt = ar[:, 6144:7168].rearrange("p (n q t) -> p n q t", n=2, q=2)
        madd, mcnt = ar[:, 10240:10624], ar[:, 10624:11008]
        sm = ar[:, 7936:8704].rearrange("p (n k) -> p n k", n=2)
        pt = ar[:, 8704:9472].rearrange("p (n k) -> p n k", n=2)
        at = ar[:, 9472:9984].rearrange("p (n t) -> p n t", n=2)
        xr = ar[:, 10240:12288].rearrange("p (c t) -> p c t", c=RC)
        gate = ar[:, 12288:14336].rearrange("p (c t) -> p c t", c=RC)
        xc = rtmp[:, 0, :].rearrange("p (c t) -> p c t", c=RC)
        bd = rtmp[:, 1, :].rearrange("p (m c d) -> p m c d", m=2, c=RC)
        rg = ar[:, 4096:6144].rearrange("p (c t) -> p c t", c=RC)
        ig = ar[:, 6144:8192].rearrange("p (c t) -> p c t", c=RC)
        av = ar[:, 8192:10240].rearrange("p (c t) -> p c t", c=RC)
        poly = ar[:, 10240:12288]
        naive = rtmp[:, 1, :]
        rsq = ar[:, 8192:10240]
        skey = ar[:, 4096:6144].rearrange("p (n k) -> p n k", n=HC)
        tks = ar[:, 8192:8704].rearrange("p (b n k) -> p b n k", b=TB, n=HC)
        tki = ar[:, 8704:9216].bitcast(U32).rearrange("p (b n k) -> p b n k", b=TB, n=HC)
        tkf = ar[:, 9216:9728].rearrange("p (b n k) -> p b n k", b=TB, n=HC)
        best = ar[:, 9728:9984].rearrange("p (b n k) -> p b n k", b=TB, n=PH)
        ex = ar[:, 9984:10240].rearrange("p (b n) -> p b n", b=TB)
        cand = ar[:, 10240:12288].rearrange("p (n a b) -> p n a b", n=PH, a=TOPK)
        eq = ar[:, 12288:14336].rearrange("p (n a b) -> p n a b", n=PH, a=TOPK)
        stg = [ar[:, 8192:10240], ar[:, 12288:14336]]
        gt = ar[:, 10240:12288]
        irep = ar[:, 10240:10752].bitcast(BF16).rearrange("p (i t) -> p i t", t=8)
        eqb = ar[:, 10752:11776].bitcast(BF16).rearrange("p (n i t) -> p n i t", n=2, t=8)
        fnb = ar[:, 8192:10240]
        pp = ar[:, 4096:8192].rearrange("p (b d) -> p b d", b=TB)
        pst = [ar[:, o:o + 2048].rearrange("p (b d) -> p b d", b=TB) for o in (6144, 12288)]
        bias = ar[:, 10240:12288]
        xg = ar[:, 0:4096].rearrange("p (k t) -> p k t", k=KC)
        junks = [ar[:, o:o + 4096].rearrange("p (n b d) -> p n b d", n=4, b=TB) for o in (8192, 0)]
        sg = ar[:, 12288:14336].rearrange("p (n b d) -> p n b d", n=2, b=TB)
        praw = ar[:, 10240:10752].rearrange("p (c t) -> p c t", c=2)
        ring = AHEAD * GE * S

        raw_in = [sem(f"raw_in{i}") for i in range(RAW)]
        hi_done, lo_done, unit_used = sem("hi_done"), sem("lo_done"), sem("unit_used")
        col_in, const_in, bd_in, sk_in, late_in = sem("col_in"), sem("const_in"), sem("bd_in"), sem("sk_in"), sem("late_in")
        xt_in = [sem(f"xt_in{i}") for i in range(4)]
        x_in = [sem(f"x_in{i}") for i in range(TB)]
        mask_in, diag_done, bc_ready = sem("mask_in"), sem("diag_done"), sem("bc_ready")
        xg_scaled, xg_high, pp_out = sem("xg_scaled"), sem("xg_high"), sem("pp_out")
        pre_done = sem("pre_done")
        mm_free, st_free, ua_free = sem("mm_free"), sem("st_free"), sem("ua_free")
        ssq_done = sem("ssq_done")
        xt_ready, xt_gain, xt_split = sem("xt_ready"), sem("xt_gain"), sem("xt_split")
        dve_step = sem("dve_step")
        trig_ready, sin_done = sem("trig_ready"), sem("sin_done")
        rope_done = sem("rope_done")
        ht_ready, ht_copied = sem("ht_ready"), sem("ht_copied")
        sc_ready, sc_read = sem("sc_ready"), sem("sc_read")
        nmx_done, exp_done, prob_done = sem("nmx_done"), sem("exp_done"), sem("prob_done")
        pt_ready, pt_copied = sem("pt_ready"), sem("pt_copied")
        pv_ready, pv_gain, at_split = sem("pv_ready"), sem("pv_gain"), sem("at_split")
        asum_ready, asum_out = sem("asum_ready"), sem("asum_out")
        bd_zero, conv_done, bd_ready = sem("bd_zero"), sem("conv_done"), sem("bd_ready")
        gates_done, l_done, a_done = sem("gates_done"), sem("l_done"), sem("a_done")
        rnn_split, rsum_out = sem("rnn_split"), sem("rsum_out")
        key_ready, key_read = sem("key_ready"), sem("key_read")
        bm_done, eg_done, picked = sem("bm_done"), sem("eg_done"), sem("picked")
        sel_ready = sem("sel_ready")
        hot_done, g_ready, g_copied = sem("hot_done"), sem("g_ready"), sem("g_copied")
        g_out = [sem("g_out0"), sem("g_out1")]
        g_in, g_used, wexp_done = sem("g_in"), sem("g_used"), sem("wexp_done")
        sig_done, ple_done, y_done, out_done = sem("sig_done"), sem("ple_done"), sem("y_done"), sem("out_done")
        mean_done, root_done = sem("mean_done"), sem("root_done")
        one_done, pop_done, lam_done, gelu_done = sem("one_done"), sem("pop_done"), sem("lam_done"), sem("gelu_done")
        rate_exp, rm_done, rm_gain = sem("rate_exp"), sem("rm_done"), sem("rm_gain")

        N_CONST = 4

        block = ctx.enter_context(nc.Block())

        @block.sync
        def _(sp):
            def first(b):
                sp.dma_start(raw[:, b, :], stream[b]).then_inc(raw_in[b], 16)

            first(0)
            for b in range(4):
                sp.dma_start(xtr[:, 4 * b:4 * b + 4, :], x_t[:, 4 * b:4 * b + 4, :]).then_inc(xt_in[b], 16)
                if b == 1:
                    first(1)
            first(2)
            first(3)
            for b in range(TB):
                sp.dma_start(hres[:, b, :], x[P * b:P * b + P, :]).then_inc(x_in[b], 16)
                first(4 + b)
            first(6)
            first(7)
            with sp.Fori(1, UNITS // RAW) as i:
                for b in range(RAW):
                    sp.wait_ge(lo_done, RAW * i + b - RAW + 1)
                    sp.dma_start(raw[:, b, :], stream[RAW * i + b]).then_inc(raw_in[b], 16)
            for n in range(UNITS // RAW * RAW, UNITS):
                sp.wait_ge(lo_done, n - RAW + 1)
                sp.dma_start(raw[:, n % RAW, :], stream[n]).then_inc(raw_in[n % RAW], 16)
            for b in range(TB):
                for e in range(4):
                    sp.wait_ge(y_done, 4 * b + e + 1)
                    sp.dma_start(out[P * b:P * b + P, 512 * e:512 * e + 512],
                                 xs[:, b, 512 * e:512 * e + 512]).then_inc(out_done, 16)
            sp.wait_ge(out_done, 16 * 4 * TB)

        @block.gpsimd
        def _(pool):
            pool.memset(ones[:], 1.0).then_inc(one_done, 1)
            with pool.Fori(0, UNITS // CV // 2) as i:
                for b in range(2 * CV):
                    pool.wait_ge(hi_done, 2 * CV * i + b + 1)
                    pool.tensor_tensor(lo[:, b % CV, :], raw[:, b, :], hi[:, b % CV, :].bitcast(F32),
                                       ALU.subtract).then_inc(lo_done, 1)
            for n in range(UNITS // (2 * CV) * 2 * CV, UNITS):
                pool.wait_ge(hi_done, n + 1)
                pool.tensor_tensor(lo[:, n % CV, :], raw[:, n % RAW, :], hi[:, n % CV, :].bitcast(F32),
                                   ALU.subtract).then_inc(lo_done, 1)

        @block.scalar
        def _(act):
            made = [0]

            def round_unit(n, k, loop):
                act.wait_ge(raw_in[k], 2 * (n - k) + 16)
                if loop or n >= CV:
                    act.wait_ge(unit_used, n - CV + 1)
                act.activation(hi[:, k % CV, :], raw[:, k, :], ACT.Copy).then_inc(hi_done, 1)

            def round_to(n):
                while made[0] <= min(n, UNITS - 1):
                    round_unit(made[0], made[0] % RAW, False)
                    made[0] += 1

            act.dma_start(col[:], cols).then_inc(col_in, 16)
            act.dma_start(praw, p_t).then_inc(const_in, 16)
            act.dma_start(idn[:], ident).then_inc(const_in, 16)
            act.dma_start(posi[:], positions).then_inc(const_in, 16)
            act.dma_start(iot[:], iota).then_inc(const_in, 16)

            def root(n, at_):
                act.wait_ge(mean_done, n + 1)
                act.activation(at_, at_, ACT.Sqrt).then_inc(root_done, 1)

            def squares(n, m, c):
                act.wait_ge(mm_free, m + 1)
                for b in range(TB):
                    ins = act.activation(junks[n - 1][:, c, b, :], hres[:, b, 512 * c:512 * c + 512], ACT.Square,
                                         accum_out=sml[:, 32 + 4 * b + c:33 + 4 * b + c])
                ins.then_inc(ssq_done, 1)

            def gains(n, c0, ks, src):
                for k in ks:
                    if k % 2 == 0 and n:
                        act.wait_ge(xt_ready, 8 * (n - 1) + k // 2 + 1)
                    if k % 2 == 0 and n != 1 and k >= 4:
                        act.wait_ge(xt_split, 8 * n + k // 2 - 1)
                    act.activation(xg[:, k, :] if n == 1 else tmp[:, k // 2 % 2, k % 2, :], src(k), ACT.Copy,
                                   scale=col[:, c0 + k:c0 + k + 1]).then_inc(xt_gain, 1)

            def turned(k):
                return bank[4 + k // 2 % 4][:, k % 2 * S:k % 2 * S + S]

            act.wait_ge(one_done, 1)
            act.activation(sml[:, 500:501], ones[:, 0:1], ACT.Sqrt)
            round_to(0)
            act.wait_ge(col_in, 16)
            for u in range(4):
                act.wait_ge(xt_in[u], 16)
                gains(0, C_MIX, range(4 * u, 4 * u + 4), lambda k: xtr[:, k, :])
                if u % 2 == 1:
                    round_to(1 + u // 2)
            round_to(3)
            act.wait_ge(bd_zero, 1)
            for m, w in enumerate((w_a, w_x)):
                for e in range(2):
                    act.dma_start(bd[64 * e:64 * e + 64, m, :, 64 * e:64 * e + 64],
                                  w.rearrange("(c e) i o -> e i c o", e=2)[e]).then_inc(bd_in, 16)
            act.wait_ge(xt_gain, KC)
            act.wait_ge(x_in[0], 16)
            act.activation(xs[:, 0, :], hres[:, 0, :], ACT.Square, accum_out=sml[:, 0:1]).then_inc(ssq_done, 1)
            round_to(CV + 1)
            root(0, sml[:, 8:10])
            round_to(CV + 3)
            act.wait_ge(lam_done, 1)
            act.activation(sml[:, 272:280], sml[:, 264:272], ACT.Exp, scale=-1.0).then_inc(rate_exp, 1)
            round_to(U_GATE + 3 + CV - 1)
            for n in range(2 * RC):
                m, c = n // RC, n % RC
                act.wait_ge(bd_ready, n + 1)
                act.activation((rg, ig)[m][:, c, :], bank[4 + n % 4][:, 0:S], ACT.Sigmoid,
                               bias=col[:, (C_BA, C_BX)[m] + c:(C_BA, C_BX)[m] + c + 1]).then_inc(gates_done, 1)
            round_to(U_GATE + 9 + CV - 1)
            act.wait_ge(l_done, 1)
            act.activation(ar[:, 8192:10240], ar[:, 4096:6144], ACT.Exp, scale=-1.0).then_inc(a_done, 1)
            round_to(U_GATE + 15 + CV - 1)
            act.wait_ge(st_free, 16)
            act.activation(ar[:, 12288:14336], ar[:, 12288:14336], ACT.Gelu_apprx_tanh).then_inc(gelu_done, 1)
            def beside(m, u):
                if (m, u) == (0, 1):
                    root(1, naive)
                if (m, u) == (0, 4):
                    act.wait_ge(trig_ready, 1)
                    act.activation(sml[:, 128:192], sml[:, 64:128], ACT.Sin).then_inc(sin_done, 1)
                if (m, u) == (1, 0):
                    act.wait_ge(rm_done, 1)
                    act.dma_start(madd, masks[0]).then_inc(mask_in, 16)
                    act.dma_start(mcnt, masks[1]).then_inc(mask_in, 16)
                if m == 1 and u < 4:
                    for c in (2 * u, 2 * u + 1):
                        act.activation(ig[:, c, :], gate[:, c, :], ACT.Copy,
                                       scale=col[:, C_GR + c:C_GR + c + 1]).then_inc(rm_gain, 1)
                if m == 1 and 4 <= u < 6:
                    o = 1024 * (u - 4)
                    act.activation(rsq[:, o:o + 1024], ar[:, 12288 + o:13312 + o], ACT.Square).then_inc(rm_gain, 1)
                if (m, u) == (2, 4):
                    root(2, sml[:, 26:28])

            for m in range(6):
                for u in range(8):
                    round_to(U_QKV + 8 * m + u + CV - 1)
                    beside(m, u)
                act.wait_ge(unit_used, U_QKV + 8 * m + 8)
                for b in range(TB):
                    dst = qk[:, b, 512 * m:512 * m + 512] if m < 4 else vsb[:, b, 512 * (m - 4):512 * (m - 3)]
                    ins = act.activation(dst, bank[m % 2 * 2 + b][:], ACT.Copy, scale=sml[:, 8 + b:9 + b])
                ins.then_inc(mm_free, 1)

            for i in range(HEADS + 3):
                if i in BESIDE2:
                    round_to(U_OUTR + beside1(i) + CV - 1)
                h = i
                if h < HEADS:
                    act.wait_ge(ht_ready, h + 1)
                    if h >= 2:
                        act.wait_ge(sc_ready, h - 1)
                    act.activation(ar[:, 6144 + 512 * (h % 2):6656 + 512 * (h % 2)], bank[4][:], ACT.Copy).then_inc(ht_copied, 1)
                h = i - 1
                if 0 <= h < HEADS:
                    act.wait_ge(nmx_done, h + 1)
                    act.activation(sm[:, h % 2, 0:P], sm[:, h % 2, 0:P], ACT.Exp, scale=SCALE,
                                   bias=sml[:, 16 + 2 * (h % 2):17 + 2 * (h % 2)])
                    act.activation(sm[:, h % 2, P:384], sm[:, h % 2, P:384], ACT.Exp, scale=SCALE,
                                   bias=sml[:, 17 + 2 * (h % 2):18 + 2 * (h % 2)]).then_inc(exp_done, 1)
                h = i - 2
                if 0 <= h < HEADS:
                    act.wait_ge(pt_ready, h + 1)
                    if h >= 2:
                        act.wait_ge(pv_ready, h - 1)
                    act.activation(pt[:, h % 2, :], bank[6][:, 0:384], ACT.Copy).then_inc(pt_copied, 1)
                h = i - 3
                if 0 <= h < HEADS:
                    act.wait_ge(pv_ready, h + 1)
                    if h >= 2:
                        act.wait_ge(at_split, h - 1)
                    act.activation(at[:, h % 2, :], bank[7][:, 0:S], ACT.Copy,
                                   scale=col[:, C_GA + h:C_GA + h + 1])
                    act.activation(sqt[:, h % 2, :], bank[7][:, 0:S], ACT.Square).then_inc(pv_gain, 1)
                round_to(U_OUTR + beside1(i + 1) - 1 + CV - 1)
            for c in range(4):
                for u in range(4):
                    round_to(U_OUTA + 4 * c + u + CV - 1)
                    if (c, u) == (1, 0):
                        root(3, sml[:, 24:26])
                    if c >= 1 and u == 1:
                        squares(1, M_OUTA + c - 1, c - 1)
                    if c >= 1 and u == 2:
                        gains(1, C_FFN, range(4 * c - 4, 4 * c), turned)
            act.dma_start(ar[:, 4096:6144], subkeys).then_inc(sk_in, 16)
            round_to(U_PROJ + CV - 1)
            squares(1, M_OUTA + 3, 3)
            gains(1, C_FFN, (12, 13), turned)
            root(4, sml[:, 10:12])

            def project(m):
                act.wait_ge(unit_used, U_PROJ + m + 1)
                for b in range(TB):
                    ins = act.activation(pst[m // 2][:, b, 512 * (m % 2):512 * (m % 2) + 512], bank[m % 2 * 2 + b][:], ACT.Copy)
                ins.then_inc(mm_free, 1)
                if m % 2 == 1:
                    act.wait_ge(mm_free, M_PROJ + m + 1)
                    act.dma_start(held[:, :, 512 * (m - 1):512 * (m + 1)], pst[m // 2]).then_inc(pp_out, 16)

            project(0)
            round_to(U_PROJ + CV)
            gains(1, C_FFN, (14, 15), turned)
            project(1)
            for kk in range(KC // 2):
                act.wait_ge(xg_scaled, kk + 1)
                act.activation(xop[:, 2 * kk:2 * kk + 2, 0, :], xg[:, 2 * kk:2 * kk + 2, :], ACT.Copy).then_inc(xg_high, 1)
                if kk in (1, 4):
                    project(2 + kk // 4)
                if kk in (0, 2, 5):
                    round_to(U_PROJ + CV + 1 + kk // 2)
            for j in range(HC):
                round_to(U_WQ + 2 * j + 1 + CV - 1)
                act.wait_ge(unit_used, U_WQ + 2 * j + 2)
                if j >= 2:
                    act.wait_ge(key_ready, j - 1)
                act.activation(qt[:, j % 2, :], bank[j % 4][:, 0:S], ACT.Copy).then_inc(st_free, 1)

            def gelu_tile(g, j, n0):
                act.wait_ge(unit_used, n0 + 2 * j + 2)
                start = g % AHEAD * (GE * S) + j * S
                act.activation(ar[:, bass.ds(start, S)] if not isinstance(start, int) else ar[:, start:start + S],
                               bank[4 + j % 2][:, 0:S], ACT.Gelu_apprx_tanh).then_inc(ua_free, 1)

            def ahead(g, before=None):
                n0 = U_U0 + 2 * GE * g
                for j in range(GE):
                    for e in range(2):
                        off = 2 * j + e + CV - 1
                        round_unit(n0 + off, (U_U0 + off) % RAW, True)
                    if j == 0 and before is not None:
                        before()
                    gelu_tile(g, j, n0)

            def places_free():
                act.wait_ge(key_ready, HC)
                act.wait_ge(pp_out, 32)

            ahead(0, places_free)
            act.wait_ge(bm_done, TB)
            act.activation(ex, ex, ACT.Exp).then_inc(eg_done, 1)
            ahead(1)

            def spread(g, j, first):
                n0, c = U_U0 + 2 * GE * g, GE * (g - 2) + j
                for e in range(2):
                    off = 2 * j + e + CV - 1
                    round_unit(n0 + off, (U_U0 + off) % RAW, True)
                gelu_tile(g, j, n0)
                b = j % 2
                for s in range(4):
                    act.wait_ge(g_ready, 4 * c + s + 1)
                    if s == 0 and not (first and j < 2):
                        act.wait_ge(g_out[b], 8 * (c - b))
                    act.activation(stg[b].rearrange("p (i t) -> p t i", t=16)[:, 4 * s:4 * s + 4, :],
                                   bank[s][:].rearrange("p (t i) -> p t i", t=4), ACT.Copy).then_inc(g_copied, 1)
                act.wait_ge(g_copied, 4 * c + 4)
                act.dma_start(g_dram[:, :, c * P:c * P + P].rearrange("g p x -> p g x") if isinstance(c, int)
                              else g_dram[:, :, bass.ds(c * P, P)].rearrange("g p x -> p g x"),
                              stg[b].rearrange("p (g x) -> p g x", g=NG)).then_inc(g_out[b], 16)

            for j in range(GE):
                spread(2, j, True)
            for j in range(GE):
                spread(3, j, False)

            def first_weights():
                act.wait_ge(g_out[0], 128)
                act.wait_ge(g_out[1], 128)
                act.dma_start(gt, g_dram[0]).then_inc(g_in, 16)

            ahead(AHEAD - 1, first_weights)

            def v_units(n0):
                for off in range(CV - 1, 16 + CV - 1):
                    round_unit(n0 + off, (U_U0 + off) % RAW, True)

            def next_weights(g):
                act.wait_ge(g_used, g)
                act.dma_start(gt, g_dram[bass.ds(g, 1)].rearrange("g p x -> p (g x)")).then_inc(g_in, 16)

            with act.Fori(0, NG - AHEAD) as g:
                next_weights(g + 1)
                n0 = U_VU + 32 * g
                v_units(n0)
                for j in range(GE):
                    for e in range(2):
                        off = 16 + 2 * j + e + CV - 1
                        round_unit(n0 + off, (U_U0 + off) % RAW, True)
                    gelu_tile(g + AHEAD, j, n0 + 16)
            with act.Fori(NG - AHEAD, NG - 1) as g:
                next_weights(g + 1)
                v_units(U_V1 + 16 * (g - (NG - AHEAD)))
            made[0] = U_LAST + CV - 1
            for c in range(4):
                for u in range(4):
                    round_to(U_LAST + 4 * c + u + CV - 1)
                    if c >= 1 and u == 1:
                        squares(2, M_PLE - 4 + c - 1, c - 1)
                    if c >= 1 and u == 2:
                        gains(2, C_PLE, range(4 * c - 4, 4 * c), turned)
            act.wait_ge(wexp_done, 4 * NG)
            act.dma_start(fnb, final_norm).then_inc(late_in, 16)
            act.dma_start(bias, b_gate).then_inc(late_in, 16)
            act.dma_start(pp, held).then_inc(late_in, 16)
            squares(2, M_PLE - 1, 3)

            def sigmoids(m):
                for b in range(TB):
                    act.wait_ge(pre_done, 2 * m + b + 1)
                    act.activation(sg[:, m % 2, b], sg[:, m % 2, b], ACT.Sigmoid).then_inc(sig_done, 1)

            def last_squares(m):
                for b in range(TB):
                    act.wait_ge(ple_done, 2 * m + b + 1)
                    act.activation(xs[:, b, 512 * m:512 * m + 512], hres[:, b, 512 * m:512 * m + 512], ACT.Square,
                                   accum_out=sml[:, 32 + 4 * b + m:33 + 4 * b + m]).then_inc(ssq_done, 1)

            for m in range(4):
                for u in range(8):
                    round_to(U_PLE + 8 * m + u + CV - 1)
                    if (m, u) == (0, 1):
                        gains(2, C_PLE, range(12, KC), turned)
                    if (m, u) == (0, 3):
                        root(5, sml[:, 12:14])
                    if m >= 1 and u == 1:
                        sigmoids(m - 1)
                    if m >= 1 and u == 3:
                        last_squares(m - 1)
            sigmoids(3)
            act.activation(sml[:, 500:501], ones[:, 0:1], ACT.Sqrt)
            last_squares(3)
            root(6, sml[:, 482:484])

        @block.tensor
        def _(pe):
            def wide(n, k, pair, x_of, first, last, loop=True):
                pe.wait_ge(lo_done, n + 1)
                for e in range(2):
                    xk = x_of(e)
                    for b in range(TB):
                        acc = bank[2 * pair + b][:]
                        wh, wl = hi[:, k, 512 * e:512 * e + 512], lo[:, k, 512 * e:512 * e + 512]
                        xh, xl = xk[:, 0, P * b:P * b + P], xk[:, 1, P * b:P * b + P]
                        pe.matmul(acc, xh, wh, start=first and e == 0, stop=False)
                        pe.matmul(acc, xh, wl, start=False, stop=False)
                        ins = pe.matmul(acc, xl, wh, start=False, stop=last and e == 1)
                ins.then_inc(unit_used, 1)

            def tall(n, k, acc, half, pairs=None):
                pe.wait_ge(lo_done, n + 1)
                for e in range(8):
                    if pairs is not None and e % 2 == 0:
                        pe.wait_ge(xt_split, pairs + 4 * half + e // 2 + 1)
                    xk = xop[:, 8 * half + e]
                    wh, wl = hi[:, k, P * e:P * e + P], lo[:, k, P * e:P * e + P]
                    pe.matmul(acc, wh, xk[:, 0, :], start=half == 0 and e == 0, stop=False)
                    pe.matmul(acc, wh, xk[:, 1, :], start=False, stop=False)
                    ins = pe.matmul(acc, wl, xk[:, 0, :], start=False, stop=half == 1 and e == 7)
                ins.then_inc(unit_used, 1)

            def chunk(m, n0, units, x_of, loop=False, pair=None, weights=None, beside=None):
                pair = m % 2 if pair is None else pair
                if not loop and m >= M_PLE + 2:
                    pe.wait_ge(pre_done, 2 * (m - M_PLE) - 2)
                elif loop or m >= 2:
                    pe.wait_ge(mm_free, m - 1)
                for u in range(units):
                    if weights is not None:
                        pe.wait_ge(wexp_done, weights + u + 1)
                    wide(n0 + u, ((n0 if isinstance(n0, int) else 0) + u) % CV, pair, lambda e, u=u: x_of(2 * u + e),
                         u == 0, u == units - 1)
                    if u == 1 and beside is not None:
                        beside()

            def turn(n, c):
                pe.wait_ge(mm_free, (M_PROJ, M_PLE)[n - 1] - 3 + c)
                for kk in (2 * c, 2 * c + 1):
                    if kk >= 4:
                        pe.wait_ge(xt_gain, 16 * n + 2 * kk - 6)
                    for e in range(2):
                        for b in range(TB):
                            k = 2 * kk + e
                            ins = pe.transpose(bank[4 + kk % 4][:, S * e + P * b:S * e + P * b + P],
                                               hres[:, b, P * k:P * k + P], idn[:])
                    ins.then_inc(xt_ready, 1)

            def broadcast(n):
                pe.wait_ge(diag_done, n + 1)
                if n:
                    pe.wait_ge(xt_gain, KC + 10)
                for b in range(TB):
                    ins = pe.matmul(bank[4][:, P * b:P * b + P], ones[:], grest[:, P * b:P * b + P], start=True, stop=True)
                ins.then_inc(bc_ready, 1)

            pe.wait_ge(one_done, 1)
            for j in range(2 * RC):
                if j >= 4:
                    pe.wait_ge(st_free, j - 3)
                for u in range(2):
                    tall(U_XR + 2 * j + u, (2 * j + u) % CV, bank[j % 4][:, 0:S], u, 0 if j == 0 else None)
                    if (j, u) == (3, 0):
                        broadcast(0)
                if j == RC + 1:
                    pe.wait_ge(bd_in, 64)
                    pe.wait_ge(conv_done, 1)
                    for n in range(2 * RC):
                        if n >= 4:
                            pe.wait_ge(gates_done, n - 3)
                        pe.matmul(bank[4 + n % 4][:, 0:S], bd[:, n // RC, n % RC, :], xc[:, n % RC, :],
                                  start=True, stop=True).then_inc(bd_ready, 1)
            pe.wait_ge(st_free, 16)
            chunk(0, U_QKV, 8, lambda k: xop[:, k])
            chunk(1, U_QKV + 8, 8, lambda k: xop[:, k])
            pe.wait_ge(rm_gain, RC + 2)
            sq = rsq.rearrange("p (c t) -> p c t", c=RC)
            for b in range(TB):
                for c in range(RC):
                    ins = pe.matmul(bank[7][:, 256 + 2 * b:257 + 2 * b], sq[:, c, P * b:P * b + P], ones[:, 0:1],
                                    start=c == 0, stop=c == RC - 1)
            ins.then_inc(rsum_out, 1)
            for m in range(2, 6):
                chunk(m, U_QKV + 8 * m, 8, lambda k: xop[:, k])

            def side_unit(n):
                m, u = n // 4, n % 4
                if u == 0:
                    pe.wait_ge(mm_free, M_OUTR + m - 1)
                wide(U_OUTR + n, n % CV, m % 2, lambda e: rop[:, 2 * u + e], u == 0, u == 3)

            pe.wait_ge(const_in, 16 * N_CONST)
            pe.wait_ge(rnn_split, 1)
            for i in range(HEADS + 3):
                h = i
                if h < HEADS:
                    if h == 0:
                        pe.wait_ge(rope_done, 1)
                    else:
                        pe.wait_ge(ht_copied, h)
                    for q in range(2):
                        for b in range(TB):
                            ins = pe.transpose(bank[4][:, S * q + P * b:S * q + P * b + P],
                                               qk[:, b, A * q + P * h:A * q + P * h + P], idn[:])
                    ins.then_inc(ht_ready, 1)
                if i in BESIDE2:
                    side_unit(beside1(i))
                h = i - 1
                if 0 <= h < HEADS:
                    pe.wait_ge(ht_copied, h + 1)
                    if h >= 1:
                        pe.wait_ge(sc_read, h)
                    qh, kh = qkt[:, h % 2, 0, :], qkt[:, h % 2, 1, :]
                    pe.matmul(bank[5][:, 0:P], qh[:, 0:P], kh[:, 0:P], start=True, stop=True)
                    pe.matmul(bank[5][:, P:384], qh[:, P:S], kh, start=True, stop=True).then_inc(sc_ready, 1)
                h = i - 2
                if 0 <= h < HEADS:
                    pe.wait_ge(prob_done, h + 1)
                    if h >= 1:
                        pe.wait_ge(pt_copied, h)
                    for j in range(3):
                        ins = pe.transpose(bank[6][:, P * j:P * j + P], sm[:, h % 2, P * j:P * j + P], idn[:])
                    ins.then_inc(pt_ready, 1)
                h = i - 3
                if 0 <= h < HEADS:
                    pe.wait_ge(pt_copied, h + 1)
                    pe.wait_ge(mm_free, 6)
                    if h >= 1:
                        pe.wait_ge(pv_gain, h)
                    v0, v1 = (vsb[:, b, P * h:P * h + P] for b in range(TB))
                    pr = pt[:, h % 2, :]
                    pe.matmul(bank[7][:, 0:P], v0, pr[:, 0:P], start=True, stop=True)
                    pe.matmul(bank[7][:, P:S], v0, pr[:, P:S], start=True, stop=False)
                    pe.matmul(bank[7][:, P:S], v1, pr[:, S:384], start=False, stop=True).then_inc(pv_ready, 1)
                side_unit(beside1(i + 1) - 1)

            def attended(k):
                pe.wait_ge(at_split, k + 1)
                return xop[:, GE + k]

            chunk(M_OUTA, U_OUTA, 4, attended)
            pe.wait_ge(asum_ready, 1)
            for b in range(TB):
                ins = pe.matmul(bank[7][:, 256 + 2 * b:257 + 2 * b], sqsum[:, P * b:P * b + P], ones[:, 0:1],
                                start=True, stop=True)
            ins.then_inc(asum_out, 1)
            for c in range(1, 4):
                chunk(M_OUTA + c, U_OUTA + 4 * c, 4, lambda k: xop[:, GE + k], beside=lambda: turn(1, c - 1))
            for m in range(4):
                chunk(M_PROJ + m, U_PROJ + m, 1, lambda k: pop[:, k])
                if m == 0:
                    turn(1, 3)
                if m == 1:
                    broadcast(1)

            def key_scores(j):
                pe.wait_ge(st_free, 16 + j + 1)
                if j >= 2:
                    pe.wait_ge(key_read, j - 1)
                for b in range(TB):
                    ins = pe.matmul(bank[6 + j % 2][:, P * b:P * b + P], qt[:, j % 2, P * b:P * b + P],
                                    skey[:, j, :], start=True, stop=True)
                ins.then_inc(key_ready, 1)

            for j in range(HC):
                if j >= 4:
                    pe.wait_ge(st_free, 16 + j - 3)
                elif j % 2 == 0:
                    pe.wait_ge(mm_free, M_PROJ + 3 + j // 2)
                for u in range(2):
                    tall(U_WQ + 2 * j + u, (2 * j + u) % CV, bank[j % 4][:, 0:S], u, 8 if j == 0 else None)
                if j == 0:
                    pe.wait_ge(sk_in, 16)
                if j >= 2:
                    key_scores(j - 2)
            key_scores(HC - 2)

            def expert_pair(n0, t, each=None):
                for b in range(2):
                    if not isinstance(t, int) or t + b >= 2:
                        pe.wait_ge(ua_free, t + b - 1)
                    for u in range(2):
                        tall(n0 + 2 * b + u, 2 * b + u, bank[4 + b][:, 0:S], u)
                    if each:
                        each(b)

            def spread(c, first):
                for s in range(4):
                    if s % 2 == 0:
                        pe.wait_ge(hot_done, 2 * c + s // 2 + 1)
                    if not first:
                        pe.wait_ge(g_copied, 4 * c + s - 3)
                    for k in range(4):
                        rows = hot[:, s // 2, :, :, 4 * (s % 2) + k]
                        for part in range(3):
                            ins = pe.matmul(bank[s][:, P * k:P * k + P], rows[:, 0], rows[:, 1 + part],
                                            start=part == 0, stop=part == 2)
                    ins.then_inc(g_ready, 1)

            expert_pair(U_U0, 0, lambda b: key_scores(HC - 1) if b == 0 else None)
            with pe.Fori(1, GE - 2) as i:
                expert_pair(U_U0 + 4 * i, 2 * i)
            for b in range(TB):
                pe.wait_ge(picked, b + 1)
                for q in range(3):
                    ins = pe.transpose(bank[6 + b][:, P * q:P * q + P], pick[:, b, q, :], idn[:])
                ins.then_inc(sel_ready, 1)
            for i in range(GE - 2, GE):
                expert_pair(U_U0 + 4 * i, 2 * i)
            expert_pair(U_U0 + 4 * GE, 2 * GE, lambda b: spread(b, b == 0))
            with pe.Fori(1, GE) as i:
                expert_pair(U_U0 + 4 * GE + 4 * i, 2 * GE + 2 * i, lambda b: spread(2 * i + b, False))
            with pe.Fori(0, GE // 2) as i:
                expert_pair(U_U0 + 8 * GE + 4 * i, 4 * GE + 2 * i)
            pe.wait_ge(g_copied, 64)

            def values(g, n0):
                with pe.Fori(0, 2) as q:
                    for e in range(2):
                        chunk(M_V + 4 * g + 2 * q + e, n0 + 8 * q + 4 * e, 4, lambda k: wop[:, k], True, e,
                              weights=4 * g)

            with pe.Fori(0, NG - AHEAD) as g:
                values(g, U_VU + 32 * g)
                with pe.Fori(0, GE // 2) as q:
                    expert_pair(U_VU + 32 * g + 16 + 4 * q, GE * (g + AHEAD) + 2 * q)
            with pe.Fori(NG - AHEAD, NG - 1) as g:
                values(g, U_V1 + 16 * (g - (NG - AHEAD)))
            for c in range(4):
                chunk(M_PLE - 4 + c, U_LAST + 4 * c, 4, lambda k: wop[:, k], weights=4 * (NG - 1),
                      beside=(lambda: turn(2, c - 1)) if c else None)

            def gained(k):
                pe.wait_ge(xt_split, 16 + k // 2 + 1)
                return xop[:, k]

            for m in range(4):
                chunk(M_PLE + m, U_PLE + 8 * m, 8, gained, beside=(lambda: turn(2, 3)) if m == 0 else None)

        @block.vector
        def _(dve):
            steps = [0]

            def link(ins):
                steps[0] = steps[0] + 1
                ins.then_inc(dve_step, 1)
                dve.wait_ge(dve_step, steps[0])

            def ts(out_, in_, s1, s2, op0, op1=ALU.bypass):
                return dve.tensor_scalar(out_, in_, s1, s2, op0, op1)

            def tt(out_, a_, b_, op):
                return dve.tensor_tensor(out_, a_, b_, op)

            def stt(out_, a_, s_, b_, op0, op1, **kw):
                return dve.scalar_tensor_tensor(out_, a_, s_, b_, op0, op1, **kw)

            def rstd(n, dst, src, width):
                ts(dst, src, 1.0 / width, EPS, ALU.mult, ALU.add).then_inc(mean_done, 1)
                dve.wait_ge(root_done, n + 1)
                link(dve.reciprocal(dst, dst))

            def split_pair(n, kk):
                dve.wait_ge(xt_gain, 16 * n + 2 * kk + 2)
                src = tmp[:, kk % 2]
                link(dve.tensor_copy(xop[:, 2 * kk:2 * kk + 2, 0, :], src))
                tt(xop[:, 2 * kk:2 * kk + 2, 1, :], src, xop[:, 2 * kk:2 * kk + 2, 0, :].bitcast(F32),
                   ALU.subtract).then_inc(xt_split, 1)

            def diagonal(n, r):
                for b in range(TB):
                    ins = ts(grest[:, P * b:P * b + P], idn[:], r[:, b:b + 1], None, ALU.mult)
                ins.then_inc(diag_done, 1)
                dve.wait_ge(bc_ready, n + 1)
                link(dve.tensor_copy(bc[:], bank[4][:, 0:S]))

            def scale_tile(dst, src, sem_):
                tt(dst, src, bc[:], ALU.mult).then_inc(sem_, 1)

            dve.memset(rtmp[:, 1, :], 0.0).then_inc(bd_zero, 1)
            for kk in range(KC // 2):
                split_pair(0, kk)
            dve.wait_ge(col_in, 16)
            dve.wait_ge(const_in, 16 * N_CONST)
            link(ts(sml[:, 280:288], col[:, C_LAM:C_LAM + RC], -1.0, None, ALU.mult))
            link(tt(sml[:, 264:272], col[:, C_LAM:C_LAM + RC], sml[:, 280:288], ALU.max))
            ts(sml[:, 280:288], sml[:, 280:288], 0.0, None, ALU.max).then_inc(lam_done, 1)
            link(dve.tensor_copy(pop[:, :, 0, :], praw))
            tt(pop[:, :, 1, :], praw, pop[:, :, 0, :].bitcast(F32), ALU.subtract).then_inc(pop_done, 1)
            dve.wait_ge(pop_done, 1)
            dve.wait_ge(xt_gain, KC)
            dve.wait_ge(x_in[1], 16)
            link(stt(xs[:, 1, :], hres[:, 1, :], 1.0, hres[:, 1, :], ALU.mult, ALU.mult, accum_out=sml[:, 1:2]))
            dve.wait_ge(ssq_done, 1)
            rstd(0, sml[:, 8:10], sml[:, 0:2], D)
            diagonal(0, sml[:, 8:10])
            for c in range(RC):
                dve.wait_ge(unit_used, U_XR + 2 * c + 2)
                scale_tile(xr[:, c, :], bank[c % 4][:, 0:S], st_free)
                dve.wait_ge(st_free, c + 1)
                link(ts(xc[:, c, :], xr[:, c, :], col[:, C_CW + 3 * RC + c:C_CW + 3 * RC + c + 1],
                        col[:, C_CB + c:C_CB + c + 1], ALU.mult, ALU.add))
                for k in range(TAPS - 1):
                    lag = TAPS - 1 - k
                    ins = stt(xc[:, c, lag:S], xr[:, c, 0:S - lag], col[:, C_CW + k * RC + c:C_CW + k * RC + c + 1],
                              xc[:, c, lag:S], ALU.mult, ALU.add)
                    if k < TAPS - 2:
                        link(ins)
                    elif c == RC - 1:
                        ins.then_inc(conv_done, 1)

            def gate_tile(c):
                dve.wait_ge(unit_used, U_GATE + 2 * c + 2)
                scale_tile(gate[:, c, :], bank[c % 4][:, 0:S], st_free)

            dve.wait_ge(rate_exp, 1)
            e_, z_, z2, pz = (sml[:, o:o + 8] for o in (272, 288, 296, 304))
            link(ts(z_, e_, 2.0, None, ALU.add))
            link(dve.reciprocal(z2, z_))
            link(tt(z_, e_, z2, ALU.mult))
            link(tt(z2, z_, z_, ALU.mult))
            link(ts(pz, z2, 1.0 / 17, 1.0 / 15, ALU.mult, ALU.add))
            for k in (13, 11, 9, 7, 5, 3, 1):
                link(tt(pz, pz, z2, ALU.mult))
                link(ts(pz, pz, 1.0 / k, None, ALU.add))
            link(tt(pz, pz, z_, ALU.mult))
            link(stt(pz, pz, 2.0, sml[:, 280:288], ALU.mult, ALU.add))
            rate = sml[:, 256:264]
            link(ts(rate, pz, RGLRU_C, None, ALU.mult))
            gate_tile(0)
            gate_tile(1)
            dve.wait_ge(gates_done, 2 * RC)
            lw, aw, iw, xw = ar[:, 4096:6144], ar[:, 8192:10240], ar[:, 6144:8192], rtmp[:, 0, :]
            tt(rg, rg, rate.unsqueeze(2).to_broadcast([P, RC, S]), ALU.mult).then_inc(l_done, 1)
            link(tt(iw, iw, xw, ALU.mult))
            dve.wait_ge(l_done, 1)
            yw = xw
            link(ts(yw, lw, 2.0, 0.25, ALU.mult, ALU.min))
            gate_tile(2)
            link(ts(poly, yw, -1.0 / 720, None, ALU.mult))
            for k, f in enumerate((1.0 / 120, -1.0 / 24, 1.0 / 6, -0.5, 1.0)):
                link(stt(poly, poly, f, yw, ALU.add, ALU.mult))
                if k % 2 == 1:
                    gate_tile(3 + k // 2)
            dve.wait_ge(a_done, 1)
            link(tt(naive, aw, aw, ALU.mult))
            link(ts(naive, naive, -1.0, 1.0, ALU.mult, ALU.add))
            gate_tile(5)
            link(ts(yw, yw, 0.25, None, ALU.is_lt))
            dve.copy_predicated(naive, yw.bitcast(U32), poly).then_inc(mean_done, 1)
            gate_tile(6)
            gate_tile(7)
            ang, arg, trn = sml[:, 64:128], sml[:, 192:256], sml[:, 320:384]
            link(dve.tensor_copy(sml[:, 20:22], posi[:]))
            for b in range(TB):
                link(ts(arg[:, ROT * b:ROT * b + ROT], col[:, C_FREQ:C_FREQ + ROT], sml[:, 20 + b:21 + b], None, ALU.mult))
            link(dve.tensor_copy(arg[:, 32:64], arg[:, 0:32]))
            link(ts(trn[:, 0:32], arg[:, 0:32], 1.0 / TAU, None, ALU.mult))
            link(ts(trn[:, 32:64], arg[:, 32:64], 1.0 / TAU, 0.25, ALU.mult, ALU.add))
            link(ts(trn, trn, ROUND, None, ALU.add))
            link(ts(trn, trn, ROUND, None, ALU.subtract))
            link(stt(ang, trn, -TAU1, arg, ALU.mult, ALU.add))
            link(stt(ang, trn, -TAU2, ang, ALU.mult, ALU.add))
            link(stt(ang, trn, -TAU3, ang, ALU.mult, ALU.add))
            link(ts(ang[:, 32:64], ang[:, 32:64], TAU / 4, None, ALU.add))
            ts(ang, ang, 3.1415925, -3.1415925, ALU.min, ALU.max).then_inc(trig_ready, 1)
            dve.wait_ge(root_done, 2)
            link(tt(iw, iw, naive, ALU.mult))
            for c in range(RC):
                ins = dve.tensor_tensor_scan(rg[:, c, :], av[:, c, :], ig[:, c, :], 0.0, ALU.mult, ALU.add)
            link(ins)
            dve.wait_ge(gelu_done, 1)
            tt(ar[:, 12288:14336], lw, ar[:, 12288:14336], ALU.mult).then_inc(rm_done, 1)
            dve.wait_ge(rm_gain, RC)
            for k in range(2):
                link(dve.tensor_copy(rop[:, 4 * k:4 * k + 4, 0, :], ig[:, 4 * k:4 * k + 4, :]))
                ins = tt(rop[:, 4 * k:4 * k + 4, 1, :], ig[:, 4 * k:4 * k + 4, :],
                         rop[:, 4 * k:4 * k + 4, 0, :].bitcast(F32), ALU.subtract)
            ins.then_inc(rnn_split, 1)
            dve.wait_ge(rsum_out, 1)
            rstd_a, rstd_r = sml[:, 24:26], sml[:, 26:28]
            sums = bank[7][:, 256:260].rearrange("p (b e) -> p b e", e=2)[:, :, 0]
            rstd(2, rstd_r, sums, A)

            def add_mixed(m, end, r):
                dve.wait_ge(unit_used, end)
                o = 512 * ((m - M_OUTR) % 4)
                for b in range(TB):
                    ins = stt(hres[:, b, o:o + 512], bank[m % 2 * 2 + b][:], r[:, b:b + 1], hres[:, b, o:o + 512],
                              ALU.mult, ALU.add)
                ins.then_inc(mm_free, 1)

            dve.wait_ge(mm_free, 4)
            dve.wait_ge(sin_done, 1)
            for b in range(TB):
                rows = qk[:, b, :].rearrange("p (h d) -> p h d", d=P)
                x1, x2 = rows[:, :, 0:ROT], rows[:, :, ROT:2 * ROT]
                sn = sml[:, 128 + ROT * b:144 + ROT * b].unsqueeze(1).to_broadcast([P, 16, ROT])
                cs = sml[:, 160 + ROT * b:176 + ROT * b].unsqueeze(1).to_broadcast([P, 16, ROT])
                t1, t2 = (tmp[:, b, e].rearrange("p (h d) -> p h d", d=ROT) for e in range(2))
                tt(t1, x1, sn, ALU.mult)
                link(tt(t2, x2, sn, ALU.mult))
                tt(x1, x1, cs, ALU.mult)
                link(tt(x2, x2, cs, ALU.mult))
                tt(x1, x1, t2, ALU.subtract)
                link(tt(x2, x2, t1, ALU.add))
            dve.sem_inc(rope_done, 1)

            dve.wait_ge(mask_in, 32)
            for i in range(HEADS + 3):
                for m in range(3):
                    if beside1(i) >= 4 * m + 4 > beside1(i - 1):
                        add_mixed(M_OUTR + m, U_OUTR + 4 * m + 4, rstd_r)
                h = i - 1
                if 0 <= h < HEADS:
                    dve.wait_ge(sc_ready, h + 1)
                    if h >= 2:
                        dve.wait_ge(pt_ready, h - 1)
                    s_, st = sm[:, h % 2, :], 2 * (h % 2)
                    ins = tt(s_, bank[5][:, 0:384], madd, ALU.add)
                    ins.then_inc(sc_read, 1)
                    dve.wait_ge(sc_read, h + 1)
                    dve.tensor_reduce(sml[:, 400 + st:401 + st], s_[:, 0:P], AX_X, ALU.max)
                    link(dve.tensor_reduce(sml[:, 401 + st:402 + st], s_[:, P:384], AX_X, ALU.max))
                    ts(sml[:, 16 + st:18 + st], sml[:, 400 + st:402 + st], -SCALE, None, ALU.mult).then_inc(nmx_done, 1)
                    dve.wait_ge(exp_done, h + 1)
                    stt(s_[:, 0:P], s_[:, 0:P], 1.0, mcnt[:, 0:P], ALU.mult, ALU.mult, accum_out=sml[:, 404 + st:405 + st])
                    link(stt(s_[:, P:384], s_[:, P:384], 1.0, mcnt[:, P:384], ALU.mult, ALU.mult,
                             accum_out=sml[:, 405 + st:406 + st]))
                    link(dve.reciprocal(sml[:, 408 + st:410 + st], sml[:, 404 + st:406 + st]))
                    ts(s_[:, 0:P], s_[:, 0:P], sml[:, 408 + st:409 + st], None, ALU.mult)
                    ts(s_[:, P:384], s_[:, P:384], sml[:, 409 + st:410 + st], None, ALU.mult).then_inc(prob_done, 1)
                h = i - 3
                if 0 <= h < HEADS:
                    dve.wait_ge(pv_gain, h + 1)
                    if h == 0:
                        link(dve.tensor_copy(sqsum, sqt[:, 0, :]))
                    else:
                        link(tt(sqsum, sqsum, sqt[:, h % 2, :], ALU.add))
                    link(dve.tensor_copy(xop[:, GE + h, 0, :], at[:, h % 2, :]))
                    tt(xop[:, GE + h, 1, :], at[:, h % 2, :], xop[:, GE + h, 0, :].bitcast(F32),
                       ALU.subtract).then_inc(at_split, 1)
            dve.sem_inc(asum_ready, 1)
            add_mixed(M_OUTR + 3, U_OUTR + 16, rstd_r)
            dve.wait_ge(asum_out, 1)
            rstd(3, rstd_a, sums, A)
            for c in range(4):
                add_mixed(M_OUTA + c, U_OUTA + 4 * c + 4, rstd_a)

            def mean_square(r):
                link(dve.tensor_reduce(r, sml[:, 32:40].rearrange("p (b m) -> p b m", b=TB), AX_X, ALU.add))

            dve.wait_ge(ssq_done, 1 + 4)
            mean_square(sml[:, 10:12])
            rstd(4, sml[:, 10:12], sml[:, 10:12], D)
            diagonal(1, sml[:, 10:12])

            for kk in range(KC // 2 + 1):
                if kk < KC // 2:
                    two = xg[:, 2 * kk:2 * kk + 2, :]
                    dve.wait_ge(xt_gain, KC + 2 * kk + 2)
                    tt(two, two, bc[:].unsqueeze(1).to_broadcast([P, 2, S]), ALU.mult).then_inc(xg_scaled, 1)
                if kk >= 1:
                    dve.wait_ge(xg_high, kk)
                    tt(xop[:, 2 * kk - 2:2 * kk, 1, :], xg[:, 2 * kk - 2:2 * kk, :],
                       xop[:, 2 * kk - 2:2 * kk, 0, :].bitcast(F32), ALU.subtract).then_inc(xt_split, 1)

            def top16(vals, work, last):
                for v, w_, t, ix in vals:
                    ins = dve.max(t[:, 0:8], v)
                link(ins)
                for v, w_, t, ix in vals:
                    dve.max_index(ix[:, 0:8], t[:, 0:8], v)
                for v, w_, t, ix in vals:
                    ins = dve.match_replace(w_, t[:, 0:8], v, NEG)
                if last is not None:
                    ins.then_inc(last, 1)
                    dve.wait_ge(last, last_at[0])
                else:
                    link(ins)
                for v, w_, t, ix in vals:
                    ins = dve.max(t[:, 8:16], w_)
                link(ins)
                for v, w_, t, ix in vals:
                    ins = dve.max_index(ix[:, 8:16], t[:, 8:16], w_)
                return ins

            last_at = [0]
            for j in range(HC):
                dve.wait_ge(key_ready, j + 1)
                last_at[0] = j + 1
                ins = top16([(bank[6 + j % 2][:, P * b:P * b + P], tkw[:, b, 0:P], tks[:, b, j, :], tki[:, b, j, :])
                             for b in range(TB)], None, key_read)
                if j % 2 == 1:
                    h = j // 2
                    link(ins)
                    for b in range(TB):
                        ins = tt(cand[:, 2 * (h % 2) + b], tks[:, b, j - 1, :].unsqueeze(2).to_broadcast([P, TOPK, TOPK]),
                                 tks[:, b, j, :].unsqueeze(1).to_broadcast([P, TOPK, TOPK]), ALU.add)
                    link(ins)
                    ins = top16([(cand[:, 2 * (h % 2) + b].rearrange("p a b -> p (a b)"), tkw[:, b, :], best[:, b, h, :],
                                  pos[:, b, TOPK * h:TOPK * h + TOPK]) for b in range(TB)], None, None)
                    link(ins)
            link(dve.tensor_copy(ar[:, 9216:9728], ar[:, 8704:9216].bitcast(U32)))

            dve.wait_ge(pp_out, 32)
            for b in range(TB):
                i2 = tkf[:, b].rearrange("p (h c) k -> p h c k", c=2)
                exb = ex[:, b, :].rearrange("p (h k) -> p h k", k=TOPK)
                tt(exb, best[:, b], best[:, b, :, 0:1].to_broadcast([P, PH, TOPK]), ALU.subtract).then_inc(bm_done, 1)
                qd = tmp[:, 1, :, 0:P]
                link(ts(eq[:, 0:1].rearrange("p n a b -> p (n a b)")[:, 0:P].bitcast(U32), pos[:, b, :], 4, None,
                        ALU.logical_shift_right))
                link(dve.tensor_copy(qd[:, 0, :], eq[:, 0:1].rearrange("p n a b -> p (n a b)")[:, 0:P].bitcast(U32)))
                link(ts(eq[:, 0:1].rearrange("p n a b -> p (n a b)")[:, 0:P].bitcast(U32), pos[:, b, :], 15, None,
                        ALU.bitwise_and))
                link(dve.tensor_copy(qd[:, 1, :], eq[:, 0:1].rearrange("p n a b -> p (n a b)")[:, 0:P].bitcast(U32)))
                for q in range(2):
                    flat = eq.rearrange("p n a b -> p (n a) b")
                    link(tt(flat, qd[:, q, :].unsqueeze(2).to_broadcast([P, P, TOPK]),
                            iot[:, 0:TOPK].unsqueeze(1).to_broadcast([P, P, TOPK]), ALU.is_equal))
                    link(tt(eq, eq, i2[:, :, q, :].unsqueeze(2).to_broadcast([P, PH, TOPK, TOPK]), ALU.mult))
                    link(dve.tensor_reduce(pick[:, b, q, :], flat, AX_X, ALU.add))
            dve.wait_ge(eg_done, 1)
            for b in range(TB):
                exb = ex[:, b, :].rearrange("p (h k) -> p h k", k=TOPK)
                link(dve.tensor_reduce(sml[:, 416:424], exb, AX_X, ALU.add))
                link(dve.reciprocal(sml[:, 424:432], sml[:, 416:424]))
                tt(pick[:, b, 2, :].rearrange("p (h k) -> p h k", k=TOPK), exb,
                   sml[:, 424:432].unsqueeze(2).to_broadcast([P, PH, TOPK]), ALU.mult).then_inc(picked, 1)
            dve.tensor_copy(irep, iot[:].unsqueeze(2).to_broadcast([P, P, 8]))
            for b in range(TB):
                dve.wait_ge(sel_ready, b + 1)
                dve.tensor_copy(keyb[:, :, P * b:P * b + P], bank[6 + b][:, 0:S].rearrange("p (q t) -> p q t", q=2))
                link(dve.tensor_copy(grest[:, P * b:P * b + P], bank[6 + b][:, S:384]))
            for part in range(3):
                link(dve.tensor_copy(gpart[:, part, :], grest[:]))
                if part < 2:
                    link(tt(grest[:], grest[:], gpart[:, part, :], ALU.subtract))

            def hot_rows(q, b):
                at_ = bass.ds(8 * q, 8) if not isinstance(q, int) else slice(8 * q, 8 * q + 8)
                if not isinstance(q, int) or q >= 2:
                    dve.wait_ge(g_ready, 2 * q - 2)

                def over(row):
                    return row.unsqueeze(1).to_broadcast([P, P, 8])

                tt(hot[:, b, 0], irep, over(keyb[:, 1, at_]), ALU.is_equal)
                link(tt(eqb[:, b], irep, over(keyb[:, 0, at_]), ALU.is_equal))
                for part in range(3):
                    ins = tt(hot[:, b, 1 + part], eqb[:, b], over(gpart[:, part, at_]), ALU.mult)
                ins.then_inc(hot_done, 1)

            for b in range(2):
                hot_rows(b, b)
            start = steps[0]
            with dve.Fori(1, S // 16) as i:
                steps[0] = start + 2 * (i - 1)
                for b in range(2):
                    hot_rows(2 * i + b, b)
            steps[0] = start + 2 * (S // 16 - 1)

            def weigh(g):
                dve.wait_ge(g_in, 16 * g + 16)
                a4 = ar[:, bass.ds(g % AHEAD * (GE * S), GE * S)].rearrange("p (j c t) -> p j c t", j=GE, t=16)
                tt(a4, a4, gt.rearrange("p (c j t) -> p j c t", j=GE, t=16), ALU.mult).then_inc(g_used, 1)

            def split_weights(g, n0):
                dve.wait_ge(g_used, g + 1)
                w3 = ar[:, bass.ds(g % AHEAD * (GE * S), GE * S)].rearrange("p (j t) -> p j t", t=S)
                for u in range(4):
                    if n0 is not None:
                        dve.wait_ge(unit_used, n0 + u + 1)
                    two = slice(2 * u, 2 * u + 2)
                    link(ts(wop[:, two, 0, :], w3[:, two, :], 1.0, None, ALU.mult))
                    tt(wop[:, two, 1, :], w3[:, two, :], wop[:, two, 0, :].bitcast(F32),
                       ALU.subtract).then_inc(wexp_done, 1)

            def add_values(n0, chunks):
                for c in chunks:
                    dve.wait_ge(unit_used, n0 + 4 * c + 4)
                    for b in range(TB):
                        ins = tt(hres[:, b, 512 * c:512 * c + 512], bank[c % 2 * 2 + b][:],
                                 hres[:, b, 512 * c:512 * c + 512], ALU.add)
                    ins.then_inc(mm_free, 1)

            dve.wait_ge(g_ready, 64)
            dve.wait_ge(ua_free, GE)
            weigh(0)
            split_weights(0, None)

            def between(g, n0, wait):
                add_values(n0, (0, 1))
                if wait:
                    dve.wait_ge(ua_free, GE * (g + 2))
                weigh(g + 1)
                add_values(n0, (2,))
                split_weights(g + 1, n0 + 12)
                add_values(n0, (3,))

            start = steps[0]
            with dve.Fori(0, NG - AHEAD) as g:
                steps[0] = start + 4 * g
                between(g, U_VU + 32 * g, True)
            start = start + 4 * (NG - AHEAD)
            with dve.Fori(NG - AHEAD, NG - 1) as g:
                steps[0] = start + 4 * (g - (NG - AHEAD))
                between(g, U_V1 + 16 * (g - (NG - AHEAD)), False)
            steps[0] = start + 4 * (AHEAD - 1)
            for c in range(4):
                add_values(U_LAST, (c,))
                if c >= 1:
                    split_pair(2, 2 * c - 2)
                    split_pair(2, 2 * c - 1)
            split_pair(2, 6)
            split_pair(2, 7)
            dve.wait_ge(ssq_done, 1 + 4 + 4)
            mean_square(sml[:, 12:14])
            rstd(5, sml[:, 12:14], sml[:, 12:14], D)
            dve.wait_ge(late_in, 48)
            for m in range(4):
                dve.wait_ge(unit_used, U_PLE + 8 * m + 8)
                for b in range(TB):
                    stt(sg[:, m % 2, b, :], bank[m % 2 * 2 + b][:], sml[:, 12 + b:13 + b],
                        bias[:, 512 * m:512 * m + 512], ALU.mult, ALU.add).then_inc(pre_done, 1)
                for b in range(TB):
                    g_, h_ = sg[:, m % 2, b], hres[:, b, 512 * m:512 * m + 512]
                    dve.wait_ge(sig_done, 2 * m + b + 1)
                    link(tt(g_, g_, pp[:, b, 512 * m:512 * m + 512], ALU.mult))
                    tt(h_, h_, g_, ALU.add).then_inc(ple_done, 1)
            dve.wait_ge(ssq_done, 1 + 4 + 4 + 8)
            mean_square(sml[:, 482:484])
            rstd(6, sml[:, 482:484], sml[:, 482:484], D)
            for b in range(TB):
                for e in range(4):
                    part = slice(512 * e, 512 * e + 512)
                    stt(xs[:, b, part], hres[:, b, part], sml[:, 482 + b:483 + b], fnb[:, part],
                        ALU.mult, ALU.mult).then_inc(y_done, 1)


_OUT = (1, S, D)


def wide_units(w, n0, n1):
    k, n = w.shape
    t = w.reshape(k // 256, 2, P, n // 512, 512).transpose(3, 0, 2, 1, 4)
    return t.reshape(-1, P, UW)[n0:n1]


def tall_units(w):
    k, n = w.shape
    return w.reshape(k // 1024, 8, P, n // P, P).transpose(3, 0, 2, 1, 4).reshape(-1, P, UW)


def kernel(**inputs):
    import concourse.bacc as bacc
    from concourse.bass_utils import run_bass_kernel_spmd

    a = {n: np.asarray(v) for n, v in inputs.items()}
    w_in, w_out = a["w_in"][0], a["w_out"][0]
    u, v = a["peer_u"][0], a["peer_v"][0]
    u_groups = tall_units(u.T).reshape(NG, 16, P, UW)
    v_groups = (v.reshape(NG, 4, 2, P, 4, 512).transpose(0, 4, 1, 3, 2, 5).reshape(NG, 16, P, UW))
    parts = [tall_units(w_in[:, 3 * A:]), wide_units(w_in[:, 0:3 * A], 0, 48),
             wide_units(w_out[A:], 0, 16), wide_units(w_out[0:A], 0, 16),
             wide_units(a["ple_proj"][0], 0, 4), tall_units(a["peer_wq"][0])]
    parts += [u_groups[g] for g in range(AHEAD)]
    for g in range(NG - AHEAD):
        parts += [v_groups[g], u_groups[g + AHEAD]]
    parts += [v_groups[g] for g in range(NG - AHEAD, NG)]
    parts += [wide_units(a["ple_w_gate"][0], 0, 32)]
    stream = np.concatenate(parts)

    def by_channel(t):
        return t.reshape(-1, P).T

    half = np.arange(ROT, dtype=np.float32)
    freq = (np.float32(500000.0) ** (-half * np.float32(2.0) / np.float32(2 * ROT))).astype(np.float32)
    cols = np.concatenate([by_channel(a["mix_norm"][0]), by_channel(a["ffn_norm"][0]), by_channel(a["ple_norm"][0]),
                           by_channel(a["attn_out_norm"][0]), by_channel(a["rnn_out_norm"][0]),
                           by_channel(a["conv_w"][0]), by_channel(a["conv_b"][0]), by_channel(a["rg_ba"][0]),
                           by_channel(a["rg_bx"][0]), by_channel(a["rg_lambda"][0]),
                           np.broadcast_to(freq, (P, ROT))], axis=1)
    lag = np.arange(S)[:, None] - np.arange(S)[None, :]
    count = (lag >= 0) * ((lag <= 128) * 1.0 + (lag % 4 == 0) + (lag % 16 == 0))
    count = np.concatenate([count[0:P, 0:P], count[P:]], axis=1).astype(np.float32)
    masks = np.stack([np.where(count > 0, 0.0, MASKED).astype(np.float32), count])
    arrays = {
        "stream": stream, "x": a["x"][0], "x_t": a["x"][0].T.reshape(KC, P, S).transpose(1, 0, 2),
        "positions": a["positions"][0].reshape(TB, P).T, "cols": cols, "masks": masks,
        "w_a": a["rg_wa"][0], "w_x": a["rg_wx"][0],
        "subkeys": a["peer_subkeys"][0].reshape(HC, KEYS, P).transpose(2, 0, 1).reshape(P, HC * KEYS),
        "p_t": a["p"][0, 0].T.reshape(2, P, S).transpose(1, 0, 2), "b_gate": np.broadcast_to(a["ple_b_gate"], (P, D)),
        "final_norm": np.broadcast_to(a["final_norm"], (P, D)),
        "iota": np.broadcast_to(np.arange(P, dtype=np.float32), (P, P)), "ident": np.eye(P, dtype=np.float32),
    }
    arrays = {n: np.ascontiguousarray(t) for n, t in arrays.items()}
    nc = bacc.Bacc("TRN2", target_bir_lowering=False, num_devices=1)
    aps = {n: nc.dram_tensor(f"in_{n}", t.shape, mybir.dt.from_np(t.dtype), kind="ExternalInput").ap()
           for n, t in arrays.items()}
    g_dram = nc.dram_tensor("spread", (NG, P, 16 * P), F32, kind="Internal").ap()
    held = nc.dram_tensor("held", (P, TB, D), F32, kind="Internal").ap()
    out = nc.dram_tensor("out", (S, D), F32, kind="ExternalOutput").ap()
    build(nc, **aps, g_dram=g_dram, held=held, out=out)
    r = run_bass_kernel_spmd(nc, [{f"in_{n}": t for n, t in arrays.items()}], core_ids=[0])
    return r.results[0]["out"].reshape(_OUT)
```
